# Optimizing a Trainium2 kernel written in Bass

```python
import jax, jax.numpy as jnp
from jax import lax
import numpy as np

D_MODEL = 1024
BATCH = 1
SEQ = 512
DEPTH = 1
DEC_BATCH = 8
DEC_SEQ = 1
PAST_LEN = 256
PAGE_SIZE = 128

D_HEAD = 64
A_GROUPS = 3
A_HEADS = 4
A_WINDOWS = (128, 512, 2048)
A_DILATIONS = (1, 4, 16)
B_HEADS = 8
B_LOGIT_OFFSET = -6.0
D_FF = 2816
Q_BLOCK = 128
ALIBI_MAX_EXP = 8.0
RMS_EPS = 1e-6

kernel_name = 'hybrid_dilated_stickbreak_macaron_step'

def _rms(x, g):
    x32 = x.astype(jnp.float32)
    y = x32 * lax.rsqrt(jnp.mean(x32 * x32, axis=-1, keepdims=True) + RMS_EPS)
    return (y * g.astype(jnp.float32)).astype(x.dtype)

def _half_ffn(h, g_pre, g_post, w_gate, w_up, w_down):
    u = _rms(h, g_pre)
    f = (jax.nn.silu(u @ w_gate) * (u @ w_up)) @ w_down
    return h + 0.5 * _rms(f, g_post)

def _alibi_slopes():
    n = A_GROUPS * A_HEADS
    idx = jnp.arange(1, n + 1, dtype=jnp.float32)
    return jnp.exp2(-ALIBI_MAX_EXP * idx / n).reshape(A_GROUPS, A_HEADS)

def _split_in(u, w_in):
    wa = A_GROUPS * A_HEADS * D_HEAD
    wb = B_HEADS * D_HEAD
    sizes = (wa, wa, wa, wb, wb, wb, D_MODEL, D_MODEL)
    offsets = [sum(sizes[:i + 1]) for i in range(len(sizes) - 1)]
    qa, ka, va, qb, kb, vb, ga, gb = jnp.split(u @ w_in, offsets, axis=-1)
    lead = u.shape[:-1]
    a_shape = lead + (A_GROUPS, A_HEADS, D_HEAD)
    b_shape = lead + (B_HEADS, D_HEAD)
    return (qa.reshape(a_shape), ka.reshape(a_shape), va.reshape(a_shape),
            qb.reshape(b_shape), kb.reshape(b_shape), vb.reshape(b_shape), ga, gb)

def _dilated_window_prompt(q, k, v, window, dil, slopes):
    b, s, h, dh = q.shape
    n_sub = s // dil
    nw = window // dil
    nb = -(-n_sub // Q_BLOCK)
    pad_tail = nb * Q_BLOCK - n_sub

    def to_sub(a):
        a = a.reshape(b, n_sub, dil, h, dh).transpose(0, 2, 1, 3, 4)
        return a.reshape(b * dil, n_sub, h, dh).astype(jnp.float32)

    qs, ks, vs = to_sub(q), to_sub(k), to_sub(v)
    qs = jnp.pad(qs, ((0, 0), (0, pad_tail), (0, 0), (0, 0)))
    kp = jnp.pad(ks, ((0, 0), (nw, pad_tail), (0, 0), (0, 0)))
    vp = jnp.pad(vs, ((0, 0), (nw, pad_tail), (0, 0), (0, 0)))
    kidx = jnp.arange(nb)[:, None] * Q_BLOCK + jnp.arange(Q_BLOCK + nw)[None, :]
    kw = kp[:, kidx]
    vw = vp[:, kidx]
    qw = qs.reshape(b * dil, nb, Q_BLOCK, h, dh)
    sc = jnp.einsum('znqhd,znkhd->znhqk', qw, kw) * (D_HEAD ** -0.5)
    qi = jnp.arange(Q_BLOCK)[:, None]
    kj = jnp.arange(Q_BLOCK + nw)[None, :]
    delta = qi + nw - kj
    key_sub = jnp.arange(nb)[:, None, None] * Q_BLOCK + kj[None] - nw
    valid = (delta >= 0) & (delta <= nw) & (key_sub >= 0)
    bias = -slopes[:, None, None] * (delta * dil).astype(jnp.float32)[None]
    sc = jnp.where(valid[None, :, None], sc + bias[None, None], -jnp.inf)
    lse = jax.nn.logsumexp(sc, axis=-1)
    p = jnp.exp(sc - lse[..., None])
    o = jnp.einsum('znhqk,znkhd->znqhd', p, vw).reshape(b * dil, nb * Q_BLOCK, h, dh)[:, :n_sub]
    lse = lse.transpose(0, 1, 3, 2).reshape(b * dil, nb * Q_BLOCK, h)[:, :n_sub]

    def from_sub(a):
        rest = a.shape[2:]
        return a.reshape((b, dil, n_sub) + rest).swapaxes(1, 2).reshape((b, s) + rest)

    return from_sub(o), from_sub(lse)

def _dilated_window_sample(q, k_new, v_new, buf_kv, window, dil, slopes):
    t = q.shape[1]
    lb = buf_kv.shape[1]
    nw = window // dil
    kc = jnp.concatenate([buf_kv[:, :, 0], k_new.astype(buf_kv.dtype)], axis=1).astype(jnp.float32)
    vc = jnp.concatenate([buf_kv[:, :, 1], v_new.astype(buf_kv.dtype)], axis=1).astype(jnp.float32)
    steps = jnp.arange(nw + 1)
    idx = lb + jnp.arange(t)[:, None] - steps[None, :] * dil
    valid = idx >= 0
    kg = kc[:, jnp.maximum(idx, 0)]
    vg = vc[:, jnp.maximum(idx, 0)]
    sc = jnp.einsum('nthd,ntkhd->nhtk', q.astype(jnp.float32), kg) * (D_HEAD ** -0.5)
    bias = -slopes[:, None, None] * (steps * dil).astype(jnp.float32)[None, None, :]
    sc = jnp.where(valid[None, None], sc + bias[None], -jnp.inf)
    lse = jax.nn.logsumexp(sc, axis=-1)
    p = jnp.exp(sc - lse[..., None])
    o = jnp.einsum('nhtk,ntkhd->nthd', p, vg)
    return o, lse.transpose(0, 2, 1)

def _combine_groups(outs, lses):
    w = jax.nn.softmax(jnp.stack(lses, axis=0), axis=0)
    return jnp.sum(w[..., None] * jnp.stack(outs, axis=0), axis=0)

def _stick_breaking(q, k, v, q_pos, k_pos, b_sb):
    z = jnp.einsum('bqhd,bkhd->bhqk', q.astype(jnp.float32), k.astype(jnp.float32)) * (D_HEAD ** -0.5)
    z = z + b_sb.astype(jnp.float32)[None, :, None, None]
    causal = k_pos[None, :] < q_pos[:, None]
    log_keep = jnp.where(causal, jax.nn.log_sigmoid(-z), 0.0)
    after = lax.cumsum(log_keep, axis=3, reverse=True) - log_keep
    w = jnp.where(causal, jnp.exp(jax.nn.log_sigmoid(z) + after), 0.0)
    return jnp.einsum('bhqk,bkhd->bqhd', w, v.astype(jnp.float32))

def _stick_breaking_prompt(q, k, v, b_sb):
    b, s = q.shape[:2]
    nb = s // Q_BLOCK
    k_pos = jnp.arange(s)

    def block(i):
        start = i * Q_BLOCK
        qb = lax.dynamic_slice_in_dim(q, start, Q_BLOCK, axis=1)
        return _stick_breaking(qb, k, v, start + jnp.arange(Q_BLOCK), k_pos, b_sb)

    o = lax.map(block, jnp.arange(nb))
    return jnp.moveaxis(o, 0, 1).reshape(b, s, B_HEADS, D_HEAD)

def _stick_breaking_sample(q, k_new, v_new, pool, page_table, b_sb):
    n, n_pages = page_table.shape
    past_len = n_pages * PAGE_SIZE
    past = pool[page_table].reshape(n, past_len, 2, B_HEADS, D_HEAD)
    kc = jnp.concatenate([past[:, :, 0], k_new.astype(past.dtype)], axis=1)
    vc = jnp.concatenate([past[:, :, 1], v_new.astype(past.dtype)], axis=1)
    t = q.shape[1]
    return _stick_breaking(q, kc, vc, past_len + jnp.arange(t), jnp.arange(past_len + t), b_sb)

def _merge(h, oa, ob, ga, gb, p_a, p_b, w_o, g_post):
    lead = h.shape[:-1]
    ya = oa.reshape(lead + (A_HEADS * D_HEAD,)).astype(h.dtype) @ p_a
    yb = ob.reshape(lead + (B_HEADS * D_HEAD,)).astype(h.dtype) @ p_b
    m = jax.nn.sigmoid(ga) * ya + jax.nn.sigmoid(gb) * yb
    return h + _rms(m @ w_o, g_post)

def _prompt_mixer(qa, ka, va, qb, kb, vb, b_sb):
    b, s = qa.shape[:2]
    slopes = _alibi_slopes()
    outs, lses, bufs = [], [], []
    for g in range(A_GROUPS):
        o, lse = _dilated_window_prompt(qa[:, :, g], ka[:, :, g], va[:, :, g],
                                        A_WINDOWS[g], A_DILATIONS[g], slopes[g])
        outs.append(o)
        lses.append(lse)
        keep = min(A_WINDOWS[g], s)
        bufs.append(jnp.stack([ka[:, s - keep:, g], va[:, s - keep:, g]], axis=2))
    oa = _combine_groups(outs, lses)
    ob = _stick_breaking_prompt(qb, kb, vb, b_sb)
    pages = jnp.stack([kb, vb], axis=2).reshape(b, s // PAGE_SIZE, PAGE_SIZE, 2, B_HEADS, D_HEAD)
    return oa, ob, bufs, pages

def _sample_mixer(qa, ka, va, qb, kb, vb, a_bufs, pool, page_table, b_sb):
    slopes = _alibi_slopes()
    outs, lses, rows = [], [], []
    for g in range(A_GROUPS):
        o, lse = _dilated_window_sample(qa[:, :, g], ka[:, :, g], va[:, :, g], a_bufs[g],
                                        A_WINDOWS[g], A_DILATIONS[g], slopes[g])
        outs.append(o)
        lses.append(lse)
        rows.append(jnp.stack([ka[:, :, g], va[:, :, g]], axis=2))
    oa = _combine_groups(outs, lses)
    ob = _stick_breaking_sample(qb, kb, vb, pool, page_table, b_sb)
    b_rows = jnp.stack([kb, vb], axis=2)
    return oa, ob, rows, b_rows

def setup_inputs(seed: int = 0) -> dict:
    key = jax.random.key(seed)
    ks = iter(jax.random.split(key, 32))
    f32 = jnp.float32

    def normal(shape, scale):
        return scale * jax.random.normal(next(ks), shape, f32)

    def gain():
        return 1.0 + normal((DEPTH, D_MODEL), 0.05)

    n_pages = PAST_LEN // PAGE_SIZE
    n_used = DEC_BATCH * n_pages
    n_phys = (5 * n_used + 3) // 4
    wa = A_GROUPS * A_HEADS * D_HEAD
    wb = B_HEADS * D_HEAD
    w_in_cols = 3 * wa + 3 * wb + 2 * D_MODEL

    inputs = {}
    inputs['x_prompt'] = normal((BATCH, SEQ, D_MODEL), 1.0)
    inputs['x_sample'] = normal((DEC_BATCH, DEC_SEQ, D_MODEL), 1.0)
    inputs['cache_a1_kv'] = normal((DEPTH, DEC_BATCH, min(A_WINDOWS[0], PAST_LEN), 2, A_HEADS, D_HEAD), 1.0)
    inputs['cache_a2_kv'] = normal((DEPTH, DEC_BATCH, min(A_WINDOWS[1], PAST_LEN), 2, A_HEADS, D_HEAD), 1.0)
    inputs['cache_a3_kv'] = normal((DEPTH, DEC_BATCH, min(A_WINDOWS[2], PAST_LEN), 2, A_HEADS, D_HEAD), 1.0)
    inputs['cache_b_kv'] = normal((DEPTH, n_phys, PAGE_SIZE, 2, B_HEADS, D_HEAD), 1.0)
    perm = jax.random.permutation(next(ks), n_phys)
    inputs['page_table'] = perm[:n_used].reshape(DEC_BATCH, n_pages).astype(jnp.int32)
    inputs['g_ffn1_pre'] = gain()
    inputs['g_ffn1_post'] = gain()
    inputs['w1_gate'] = normal((DEPTH, D_MODEL, D_FF), D_MODEL ** -0.5)
    inputs['w1_up'] = normal((DEPTH, D_MODEL, D_FF), D_MODEL ** -0.5)
    inputs['w1_down'] = normal((DEPTH, D_FF, D_MODEL), D_FF ** -0.5)
    inputs['g_mix_pre'] = gain()
    inputs['g_mix_post'] = gain()
    inputs['w_in'] = normal((DEPTH, D_MODEL, w_in_cols), D_MODEL ** -0.5)
    inputs['b_sb'] = B_LOGIT_OFFSET + normal((DEPTH, B_HEADS), 0.5)
    inputs['p_a'] = normal((DEPTH, A_HEADS * D_HEAD, D_MODEL), (A_HEADS * D_HEAD) ** -0.5)
    inputs['p_b'] = normal((DEPTH, wb, D_MODEL), wb ** -0.5)
    inputs['w_o'] = normal((DEPTH, D_MODEL, D_MODEL), D_MODEL ** -0.5)
    inputs['g_ffn2_pre'] = gain()
    inputs['g_ffn2_post'] = gain()
    inputs['w2_gate'] = normal((DEPTH, D_MODEL, D_FF), D_MODEL ** -0.5)
    inputs['w2_up'] = normal((DEPTH, D_MODEL, D_FF), D_MODEL ** -0.5)
    inputs['w2_down'] = normal((DEPTH, D_FF, D_MODEL), D_FF ** -0.5)
    return inputs

def reference(x_prompt, x_sample, cache_a1_kv, cache_a2_kv, cache_a3_kv, cache_b_kv, page_table,
              g_ffn1_pre, g_ffn1_post, w1_gate, w1_up, w1_down,
              g_mix_pre, g_mix_post, w_in, b_sb, p_a, p_b, w_o,
              g_ffn2_pre, g_ffn2_post, w2_gate, w2_up, w2_down):
    hp, hs = x_prompt, x_sample
    a_caches = (cache_a1_kv, cache_a2_kv, cache_a3_kv)
    new_ap = [[] for _ in range(A_GROUPS)]
    new_as = [[] for _ in range(A_GROUPS)]
    new_bp, new_bs = [], []
    for layer in range(DEPTH):
        ffn1 = (g_ffn1_pre[layer], g_ffn1_post[layer], w1_gate[layer], w1_up[layer], w1_down[layer])
        ffn2 = (g_ffn2_pre[layer], g_ffn2_post[layer], w2_gate[layer], w2_up[layer], w2_down[layer])
        out_w = (p_a[layer], p_b[layer], w_o[layer], g_mix_post[layer])

        hp = _half_ffn(hp, *ffn1)
        qa, ka, va, qb, kb, vb, ga, gb = _split_in(_rms(hp, g_mix_pre[layer]), w_in[layer])
        oa, ob, bufs, pages = _prompt_mixer(qa, ka, va, qb, kb, vb, b_sb[layer])
        hp = _merge(hp, oa, ob, ga, gb, *out_w)
        hp = _half_ffn(hp, *ffn2)
        for g in range(A_GROUPS):
            new_ap[g].append(bufs[g])
        new_bp.append(pages)

        hs = _half_ffn(hs, *ffn1)
        qa, ka, va, qb, kb, vb, ga, gb = _split_in(_rms(hs, g_mix_pre[layer]), w_in[layer])
        a_bufs = [a_caches[g][layer] for g in range(A_GROUPS)]
        oa, ob, rows, b_rows = _sample_mixer(qa, ka, va, qb, kb, vb, a_bufs, cache_b_kv[layer],
                                             page_table, b_sb[layer])
        hs = _merge(hs, oa, ob, ga, gb, *out_w)
        hs = _half_ffn(hs, *ffn2)
        for g in range(A_GROUPS):
            new_as[g].append(rows[g])
        new_bs.append(b_rows)

    return (hp, hs,
            jnp.stack(new_ap[0]), jnp.stack(new_as[0]),
            jnp.stack(new_ap[1]), jnp.stack(new_as[1]),
            jnp.stack(new_ap[2]), jnp.stack(new_as[2]),
            jnp.stack(new_bp), jnp.stack(new_bs))


_drawn_inputs = setup_inputs


def setup_inputs(seed=0):
    import zlib

    import numpy as np

    out = dict(_drawn_inputs(seed))
    spreads = {}
    factors = {'g_ffn2_post': 3.739}
    for name, (base, spread) in spreads.items():
        noise = np.random.default_rng([zlib.crc32(name.encode()), seed]).standard_normal(out[name].shape)
        drawn = base * np.exp(spread * noise) if base else spread * noise
        out[name] = __import__('jax').numpy.asarray(drawn.astype(out[name].dtype))
    for name, factor in factors.items():
        out[name] = (out[name] * factor).astype(out[name].dtype)
    return out
```

```python
from contextlib import ExitStack

import concourse.bass as bass
from concourse import mybir

F32 = mybir.dt.float32
F32R = mybir.dt.float32r
I32 = mybir.dt.int32
ALU = mybir.AluOpType
ACT = mybir.ActivationFunctionType
AX = mybir.AxisListType

P = 128
D = 1024
KD = D // P
SEQ = 512
NB = SEQ // P
DEC = 8
T = SEQ + DEC
G = 2
TG = T // G
FF = 2816
CW = 256
CH = KD * CW
UPS = FF // CW
KF = FF // P
DNS = D // CW
KC = -(-KF // KD)
DH = 64
AG, AH, BH = 3, 4, 8
WA, WB = AG * AH * DH, BH * DH
DIL = (1, 4, 16)
PAST = 256
EPS = 1e-6
SCALE = DH ** -0.5
FAR = 1e30

FFN1, QKV, GA, GB, PA, PB, WO, FFN2 = 0, 34, 49, 53, 57, 58, 60, 64
CHUNKS = 98
R_FFN1, R_QKV, R_GA, R_GB, R_PA, R_PB, R_WO, R_FFN2 = 0, 26, 41, 45, 49, 53, 57, 61


def slope(g, h):
    return 2.0 ** (-8.0 * (g * AH + h + 1) / (AG * AH))


class Placed:

    def __init__(self, nc, at):
        self.nc, self.at = nc, at

    def __call__(self, name, shape, dt=F32):
        n = 4
        for s in shape[1:]:
            n *= s
        t = self.nc.alloc_sbuf_tensor_at(name, shape, dt, offset=self.at)
        self.at += -(-n // 32) * 32
        return t


def step_program(nc, w_stream, x_t, gains_in, b_rows, consts, sample_bias, ka_cache, va_cache1,
                 va_cache2, kb_pool, vb_pool, pages, y_t, ka1_t, ka2_t, ka3_t, kb_t, va1_o, va2_o,
                 va3_o, vb_o, vs_t):
    base = -(-nc.sbuf_base // 32) * 32
    perm = Placed(nc, base)
    h = perm("h", [P, KD, T])
    w_hi = perm("w_hi", [P, 2, CH], F32R)
    w_lo = perm("w_lo", [P, 2, CH], F32R)
    raw = perm("raw", [P, 2, CH])
    u_hi = perm("u_hi", [P, KD, T], F32R)
    f = Placed(nc, perm.at)("f", [P, KD, T])
    u_lo = perm("u_lo", [P, KD, T], F32R)
    cst = perm("cst", [P, 2 * P])
    gain = perm("gain", [P, 6, KD])
    bias_b = perm("bias_b", [P, BH + 1])
    eps = perm("eps", [P, 1])
    stat = perm("stat", [P, 16])
    tmp = perm("tmp", [P, 2, TG])
    sqa = perm("sqa", [P, 4, TG])
    sqb = perm("sqb", [P, 2, TG])
    acc = perm("acc", [P, G, TG])
    root = perm("root", [P, G, TG])
    rinv = perm("rinv", [P, G, TG])
    pg = perm("pg", [P, 2 * DEC], I32)
    ident, ones = cst[:, 0:P], cst[:, P:2 * P]
    R = perm.at
    ffn = Placed(nc, R)
    hid_hi = ffn("hid_hi", [P, KF, T], F32R)
    hid_lo = ffn("hid_lo", [P, KF, T], F32R)
    sg = ffn("sg", [P, 4, TG])
    mix = Placed(nc, R)
    oa_hi = mix("oa_hi", [P, 2, T], F32R)
    oa_lo = mix("oa_lo", [P, 2, T], F32R)
    q_a = mix("q_a", [P, 6, T])
    k_a = mix("k_a", [P, 6, T])
    v_a = mix("v_a", [P, NB, WA])
    vt = mix("vt", [P, 2, T])
    v_self = mix("v_self", [DEC, WA])
    k_self = mix("k_self", [P, 6, DEC])
    qz_a = mix("qz_a", [P, 6, DEC, AH])
    qz_b = mix("qz_b", [P, 4, DEC, BH])
    dist1 = mix("dist1", [P, 520])
    dist2 = mix("dist2", [P, P])
    dist3 = mix("dist3", [P, P])
    tri = mix("tri", [P, P])
    work = mix.at
    sc = mix("sc", [P, 2, 768])
    p_t = mix("p_t", [P, 2, 768])
    q_b = mix("q_b", [P, 4, T])
    k_b = mix("k_b", [P, 4, T])
    v_b = mix("v_b", [P, NB, WB])
    spare = mix.at
    late = Placed(nc, R + 8320)
    ob_hi = late("ob_hi", [P, 4, T], F32R)
    ob_lo = late("ob_lo", [P, 4, T], F32R)
    gate_a = late("gate_a", [P, KD, T])
    m_at = late.at
    ring = [late(f"ring{i}", [P, 512]) for i in range(3)] + [Placed(nc, spare)("ring3", [P, 512])]
    late = Placed(nc, work)
    beta = late("beta", [P, 2, 512])
    suffix = late("suffix", [P, 520])
    w_t = late("w_t", [P, 2, 512])
    keep = sqb[:, :, :].rearrange("p a b -> p (a b)")[:, 0:512]
    values = Placed(nc, work)
    va_1 = values("va_1", [P, DEC, 256])
    va_23 = values("va_23", [83, DEC, 256])
    blocks = ring + [Placed(nc, work + 2048 * i)(f"block{i}", [P, 512]) for i in range(8)]
    s_a = Placed(nc, R + 54784)("s_a", [P, 2, 211])
    flat = lambda t: t[:, :, :].rearrange("p a b -> p (a b)")
    s_beta = flat(sqa)[:, 0:512].rearrange("p (r k) -> p r k", r=2)
    s_keep = flat(sqa)[:, 512:1024].rearrange("p (r k) -> p r k", r=2)
    s_suffix = flat(tmp)[:, 0:514].rearrange("p (r k) -> p r k", r=2)
    pt_a = flat(acc)[:, 0:512].rearrange("p (n c) -> p n c", c=P)
    pt_b = flat(root)[:, 0:512].rearrange("p (n c) -> p n c", c=P)
    folded = [flat(tmp)[:, 0:512], flat(sqa)[:, 0:512], flat(sqa)[:, 512:1024]]
    end = Placed(nc, m_at)
    m_hi = end("m_hi", [P, KD, T], F32R)
    m_lo = end("m_lo", [P, KD, T], F32R)
    gate_b = end("gate_b", [P, KD, T])
    assert dist1 is not None and max(ffn.at, spare + 2048, end.at) <= nc.sbuf_usable_end

    m_tmp = [tmp[:, 0, :], tmp[:, 1, :], sqb[:, 0, :], sqb[:, 1, :]]

    psum = [nc.alloc_psum_tensor(f"bank{i}", [P, 512], F32) for i in range(8)]
    bank = psum[0:4]
    sum_post, sum_pre = psum[4:6], psum[6:8]
    s1, s2, tb, ob = psum[4:8]

    ctx = ExitStack()

    def sem(name):
        return ctx.enter_context(nc.semaphore(name))

    with ctx:
        const_in = sem("const_in")
        x_in = [sem(f"x_in{i}") for i in range(4)]
        raw_in = [sem("raw_in0"), sem("raw_in1")]
        hi_made = sem("hi_made")
        lo_made = sem("lo_made")
        part_used = sem("part_used")
        full = [sem(f"full{b}") for b in range(4)]
        read = [sem(f"read{b}") for b in range(4)]
        consts_ready = sem("consts_ready")
        hid_made = sem("hid_made")
        post_sq = sem("post_sq")
        acc_added = sem("acc_added")
        post_summed = sem("post_summed")
        h_sq = sem("h_sq")
        h_summed = sem("h_summed")
        root_made = sem("root_made")
        h_ready = sem("h_ready")
        hn_made = sem("hn_made")
        uh_made = sem("uh_made")
        u_made = sem("u_made")
        mix_in = sem("mix_in")
        mix_ready = sem("mix_ready")
        v_turned = sem("v_turned")
        v_placed = sem("v_placed")
        a_scored = sem("a_scored")
        a_biased = sem("a_biased")
        a_max = sem("a_max")
        a_exp = sem("a_exp")
        a_prob = sem("a_prob")
        a_turned = sem("a_turned")
        a_pt_act = sem("a_pt_act")
        a_pt_dve = sem("a_pt_dve")
        a_out = sem("a_out")
        a_hi = sem("a_hi")
        a_lo = sem("a_lo")
        b_scored = sem("b_scored")
        b_beta = sem("b_beta")
        b_weight = sem("b_weight")
        b_turned = sem("b_turned")
        b_wt = sem("b_wt")
        b_out = sem("b_out")
        b_hi = sem("b_hi")
        b_lo = sem("b_lo")
        ring_in = [sem(f"ring_in{i}") for i in range(4)]
        page_in = [sem(f"page_in{i}") for i in range(8)]
        ring_used = sem("ring_used")
        va_in = sem("va_in")
        va_used = sem("va_used")
        fold_copied = sem("fold_copied")
        fold_turned = sem("fold_turned")
        self_in = sem("self_in")
        s_zero = sem("s_zero")
        s_scored = sem("s_scored")
        s_bias = sem("s_bias")
        s_max = sem("s_max")
        s_exp = sem("s_exp")
        s_sig = sem("s_sig")
        s_prob = sem("s_prob")
        s_turned = sem("s_turned")
        s_pt = sem("s_pt")
        sb_out = sem("sb_out")
        s_hi = sem("s_hi")
        s_lo = sem("s_lo")
        pool_own = sem("pool_own")
        qz_made = sem("qz_made")
        m_sum = sem("m_sum")
        m_top = sem("m_top")
        m_made = sem("m_made")
        vs_out = sem("vs_out")
        ka_out = sem("ka_out")
        kb_out = sem("kb_out")
        va_out = sem("va_out")
        vb_out = sem("vb_out")
        stored = sem("stored")
        block = ctx.enter_context(nc.Block())

        def tg(g):
            return slice(g * TG, (g + 1) * TG)

        def out_of(b):
            return bank[b][:, 0:TG]

        def fold_view(src, n):
            return src[:].rearrange("p (t r j c) -> p t r j c", t=n, r=4 // n, c=32)

        def sample_columns(dst, r=None):
            s0 = SEQ if r is None else SEQ + 4 * r
            s1_ = T if r is None else s0 + 4
            return dst[:, 0:2 if r is None else 4, s0:s1_].rearrange("p t (r j) -> p t r j", j=4)

        def wait_chunk_used(eng, n):
            if n < FFN1 + 2 * UPS:
                eng.wait_ge(full[3], R_FFN1 + n - FFN1 + 1)
            elif n < QKV:
                r, kc = divmod(n - 2 * UPS, KC)
                if kc < KC - 1:
                    eng.wait_ge(part_used, (KC - 1) * r + kc + 1)
                else:
                    eng.wait_ge(full[3], R_FFN1 + 2 * UPS + r + 1)
            elif n < PA:
                eng.wait_ge(full[3], R_QKV + n - QKV + 1)
            elif n == PA:
                eng.wait_ge(full[3], R_PA + 4)
            elif n < WO:
                eng.wait_ge(full[3], R_PB + 2 * (n - PB) + 2)
            elif n < FFN2:
                eng.wait_ge(full[3], R_WO + n - WO + 1)
            elif n < FFN2 + 2 * UPS:
                eng.wait_ge(full[3], R_FFN2 + n - FFN2 + 1)
            else:
                r, kc = divmod(n - FFN2 - 2 * UPS, KC)
                if kc < KC - 1:
                    eng.wait_ge(part_used, (KC - 1) * (DNS + r) + kc + 1)
                else:
                    eng.wait_ge(full[3], R_FFN2 + 2 * UPS + r + 1)

        def post_root(p, g):
            return 3 + 4 * p + 2 * g if p < 2 else 11 + g

        def pre_root(q, g):
            return g + 1 if q == 0 else 4 * q + 2 * g

        def rounds_before_post(p):
            return 4 * p

        def m2_pieces(u):
            return [3 * (u // 2), 3 * (u // 2) + 1] if u % 2 == 0 else [3 * (u // 2) + 2]

        @block.sync
        def _(sp):
            def load(n, slot, size=CH):
                src = w_stream[n] if isinstance(n, int) else w_stream[bass.ds(n, 1)].rearrange("a p c -> (a p) c")
                sp.dma_start(raw[:, slot, 0:size], src[:, 0:size]).then_inc(raw_in[slot], 16)

            def load_next(n):
                if n >= CHUNKS:
                    return
                sp.wait_ge(lo_made, n - 1)
                start = FFN1 if n < QKV else FFN2
                down = n - start - 2 * UPS
                short = down >= 0 and (n < QKV or n >= FFN2) and down % KC == KC - 1
                load(n, n % 2, (KF - KD * (KC - 1)) * CW if short else CH)

            def ffn_loads(n0):
                with sp.Fori(0, UPS - 1) as i:
                    for s in range(2):
                        sp.wait_ge(lo_made, n0 + 2 * i + 1 + s)
                        load(n0 + 2 * i + 2 + s, s)
                for n in range(n0 + 2 * UPS, n0 + 2 * UPS + DNS * KC):
                    load_next(n)

            for s in range(4):
                sp.dma_start(h[:, 2 * s:2 * s + 2, :], x_t[:, 2 * s:2 * s + 2, :]).then_inc(x_in[s], 16)
                if s == 0:
                    sp.dma_start(cst[:], consts[:, 0:2 * P]).then_inc(const_in, 16)
                    sp.dma_start(gain[:], gains_in).then_inc(const_in, 16)
                    sp.dma_start(bias_b[:], b_rows).then_inc(const_in, 16)
                    sp.dma_start(pg[0:1, :], pages).then_inc(const_in, 16)
                if s == 1:
                    load(0, 0)
            load(1, 1)
            ffn_loads(FFN1)
            load_next(QKV)
            load_next(QKV + 1)
            sp.wait_ge(full[3], R_QKV)
            at = 2 * P
            for table, width in ((dist1, 515), (dist2, P), (dist3, P), (tri, P)):
                sp.dma_start(table[:, 0:width], consts[:, at:at + width]).then_inc(mix_in, 16)
                at += width

            def store_k(c):
                sp.wait_ge(read[3], R_QKV + c + 1)
                if c == 3:
                    sp.dma_start(ka1_t, k_a[:, 0:2, SEQ - P:T]).then_inc(ka_out, 16)
                elif c < 6:
                    out = ka2_t if c == 4 else ka3_t
                    sp.dma_start(out, k_a[:, 2 * (c - 3):2 * (c - 3) + 2, :]).then_inc(ka_out, 16)
                else:
                    j = 2 * (c - 11)
                    sp.dma_start(kb_t[:, j:j + 2, :], k_b[:, j:j + 2, :]).then_inc(kb_out, 16)

            def store_v_sample(n, c):
                sp.wait_ge(read[3], R_QKV + c + 1)
                sp.dma_start(vs_t[:, 2 * n:2 * n + 2, :], vt[:, :, SEQ:T]).then_inc(vs_out, 16)

            def store_v(n):
                sp.wait_ge(v_placed, 3 * (n + 1) if n < 3 else 9 + 2 * (n - 2))
                if n == 0:
                    sp.dma_start(va1_o, v_a[:, NB - 1, 0:256]).then_inc(va_out, 16)
                elif n < 3:
                    out = va2_o if n == 1 else va3_o
                    sp.dma_start(out, v_a[:, :, n * 256:(n + 1) * 256]).then_inc(va_out, 16)
                else:
                    j = (n - 3) * 256
                    sp.dma_start(vb_o[:, :, j:j + 256], v_b[:, :, j:j + 256]).then_inc(vb_out, 16)

            for n in range(QKV + 2, GB):
                load_next(n)
                c = n - QKV - 3
                if c in (3, 4, 5, 11, 12):
                    store_k(c)
                if c in (6, 7, 8, 13, 14):
                    v = c - 6 if c < 9 else c - 10
                    store_v_sample(v, c)
                if c in (7, 8, 9, 14, 15):
                    store_v(c - 7 if c < 10 else c - 11)
            sp.wait_ge(const_in, 64)
            def page(pool_t, x, slot, sem_in):
                r = sp.value_load(pg[0:1, x:x + 1], min_val=0, max_val=kb_pool.shape[0] - 1)
                sp.dma_start(slot[:], pool_t[bass.ds(r, 1)].rearrange("a p c -> (a p) c")).then_inc(sem_in, 16)

            def load_keys(x):
                if x >= 4:
                    sp.wait_ge(ring_used, x - 3)
                if x < DEC:
                    sp.dma_start(ring[x % 4][:, 0:422], ka_cache[x]).then_inc(ring_in[x % 4], 16)
                else:
                    page(kb_pool, x - DEC, ring[x % 4], ring_in[x % 4])

            def load_value_pages(x0, x1):
                for x in range(x0, x1):
                    if x < 4:
                        sp.wait_ge(ring_used, 21 + x)
                    elif x == 4:
                        sp.wait_ge(va_used, 1)
                    elif x >= 12:
                        sp.wait_ge(ring_used, 25 + x - 12)
                    page(vb_pool, x, blocks[x % 12], ring_in[x] if x < 4 else (page_in[x - 4] if x < 12 else ring_in[x - 12]))

            load_next(GB)
            load_next(GB + 1)
            sp.wait_ge(v_turned, 13)
            sp.wait_ge(vs_out, 80)
            sp.wait_ge(va_out, 48)
            sp.wait_ge(a_biased, AH * 4 * 3)
            sp.dma_start(s_a[:, :, :].rearrange("p r k -> p (r k)"), sample_bias).then_inc(s_bias, 16)
            for x in range(4):
                load_keys(x)
            for x in range(4, 12):
                load_keys(x)
            sp.wait_ge(b_out, 32)
            sp.wait_ge(kb_out, 32)
            sp.dma_start(va_1[:], va_cache1).then_inc(va_in, 16)
            sp.dma_start(va_23[1:65], va_cache2[0:64]).then_inc(va_in, 16)
            sp.dma_start(va_23[66:82], va_cache2[64:80]).then_inc(va_in, 16)
            for g, row in enumerate((0, 65, 82)):
                sp.dma_start(va_23[row:row + 1], v_self[:, g * 256:(g + 1) * 256]).then_inc(va_in, 16)
            load_next(GB + 2)
            for x in range(12, 20):
                load_keys(x)
            load_next(GB + 3)
            for x in range(20, 24):
                load_keys(x)
            load_value_pages(0, 4)
            load_next(GB + 4)
            load_value_pages(4, 12)
            load_next(GB + 5)
            load_value_pages(12, 16)
            for n in range(GB + 6, FFN2 + 2):
                load_next(n)
            ffn_loads(FFN2)
            for g in range(G):
                for s in range(4):
                    sp.wait_ge(h_ready, 16 + 4 * g + s + 1)
                    if s % 2:
                        sp.dma_start(y_t[:, 2 * s - 2:2 * s + 2, tg(g)], h[:, 2 * s - 2:2 * s + 2, tg(g)]).then_inc(stored, 16)
            sp.wait_ge(stored, 4 * 16)
            sp.wait_ge(ka_out, 48)
            sp.wait_ge(kb_out, 32)
            sp.wait_ge(va_out, 48)
            sp.wait_ge(vb_out, 32)
            sp.wait_ge(vs_out, 80)

        @block.gpsimd
        def _(pool):
            def lo(n, slot):
                pool.wait_ge(hi_made, n + 1)
                pool.tensor_tensor(w_lo[:, slot, :], raw[:, slot, :], w_hi[:, slot, :].bitcast(F32),
                                   ALU.subtract).then_inc(lo_made, 1)

            def los(n0, n1):
                for n in range(n0, n1):
                    lo(n, n % 2)

            with pool.Fori(0, (QKV + 2) // 2) as i:
                lo(2 * i, 0)
                lo(2 * i + 1, 1)
            pool.wait_ge(full[3], R_QKV)
            pool.memset(qz_a[:], 0.0).then_inc(pool_own, 1)
            pool.memset(qz_b[:], 0.0).then_inc(pool_own, 1)
            los(QKV + 2, QKV + 5)
            los(QKV + 5, QKV + 8)
            pool.wait_ge(read[3], R_QKV + 6)
            pool.tensor_copy(k_self[:], k_a[:, :, SEQ:T]).then_inc(pool_own, 1)
            los(QKV + 8, QKV + 13)
            los(QKV + 13, GB + 2)
            pool.wait_ge(pool_own, 3)
            for b in range(DEC):
                pool.wait_ge(ring_in[b % 4], 16 * (b // 4 + 1))
                for g, col in enumerate((128, 193, 210)):
                    dst = ring[b % 4][:, 0:422].rearrange("p (t k) -> p t k", t=2)
                    pool.tensor_copy(dst[:, :, col], k_self[:, 2 * g:2 * g + 2, b]).then_inc(self_in, 1)
            lo(GB + 2, 1)
            with pool.Fori(0, (CHUNKS - GB - 3) // 2) as i:
                lo(2 * i + GB + 3, 0)
                lo(2 * i + GB + 4, 1)

        @block.scalar
        def _(act):
            def hi_copy(slot):
                act.activation(w_hi[:, slot, :], raw[:, slot, :], ACT.Copy).then_inc(hi_made, 1)

            def hi(n):
                if n >= CHUNKS:
                    return
                act.wait_ge(raw_in[n % 2], 16 * (n // 2 + 1))
                if n >= 2:
                    wait_chunk_used(act, n - 2)
                hi_copy(n % 2)

            def square_h(q, g):
                for t in range(KD):
                    c = 16 * q + 8 * g + t
                    if q == 0:
                        act.wait_ge(x_in[t // 2], 16)
                    else:
                        act.wait_ge(h_ready, 8 * (q - 1) + 4 * g + t // 2 + 1)
                    if c >= 2:
                        act.wait_ge(h_summed, c - 1)
                    act.activation(sqb[:, t % 2, :], h[:, t, tg(g)], ACT.Square).then_inc(h_sq, 1)

            def take_root(src, summed, count, g):
                act.wait_ge(summed, count)
                act.activation(root[:, g, :], src[g][:, 0:TG], ACT.Sqrt, bias=eps[:, 0:1],
                               scale=1.0 / D).then_inc(root_made, 1)

            def u_top(q, g):
                for t in range(KD):
                    if t % 2 == 0:
                        act.wait_ge(hn_made, 8 * q + 4 * g + t // 2 + 1)
                    act.activation(u_hi[:, t, tg(g)], f[:, t, tg(g)], ACT.Copy,
                                   scale=gain[:, 2 * q, t:t + 1]).then_inc(uh_made, 1)

            def square_out(r, b, n):
                act.wait_ge(full[b], r + 1)
                if n:
                    act.wait_ge(acc_added, 4 * (n - 1) + b + 1)
                act.activation(sqa[:, b, :], out_of(b), ACT.Square).then_inc(post_sq, 1)

            def boundary(p, r, n_hi):
                for g in range(G):
                    for t in range(2):
                        square_out(r, 2 * g + t, 4 * p + 3)
                    if g == 0:
                        take_root(sum_post, post_summed, 2 * p + 1, 0)
                if p < 2:
                    square_h(p + 1, 0)
                    take_root(sum_pre, h_summed, 16 * (p + 1) + 8, 0)
                    u_top(p + 1, 0)
                take_root(sum_post, post_summed, 2 * p + 2, 1)
                if p < 2:
                    square_h(p + 1, 1)
                    take_root(sum_pre, h_summed, 16 * (p + 1) + 16, 1)
                    u_top(p + 1, 1)
                hi(n_hi)

            def ffn_up(n0, r0):
                with act.Fori(0, UPS) as i:
                    for b in range(4):
                        act.wait_ge(full[b], r0 + 1 + 2 * i)
                        act.activation(sg[:, b, :], out_of(b), ACT.Silu).then_inc(read[b], 1)
                    for s in range(2):
                        act.wait_ge(raw_in[s], n0 * 8 + 32 + 16 * i)
                        act.wait_ge(full[3], r0 + 1 + s + 2 * i)
                        hi_copy(s)

            def outputs(p, r0, n0, kc):
                for r in range(DNS):
                    n = n0 + kc * r
                    for j in range(kc - 1):
                        hi(n + j + 2)
                    if r == DNS - 1:
                        boundary(p, r0 + r, n + kc + 1)
                    else:
                        for b in range(4):
                            square_out(r0 + r, b, 4 * p + r)
                        hi(n + kc + 1)

            act.wait_ge(consts_ready, 3)
            square_h(0, 0)
            take_root(sum_pre, h_summed, 8, 0)
            u_top(0, 0)
            hi(0)
            square_h(0, 1)
            take_root(sum_pre, h_summed, 16, 1)
            u_top(0, 1)
            hi(1)
            ffn_up(FFN1, R_FFN1)
            outputs(0, R_FFN1 + 2 * UPS, FFN1 + 2 * UPS, KC)

            def project_out(c, b):
                g, t = divmod(b, 2)
                act.wait_ge(full[b], R_QKV + c + 1)
                kind, j = (c // 3, c % 3) if c < 9 else ((c - 9) // 2, (c - 9) % 2)
                if kind == 2:
                    v = c - 6 if c < 9 else c - 10
                    if b == 0 and v:
                        act.wait_ge(v_turned, 3 * v if v < 4 else 11)
                        act.wait_ge(vs_out, 16 * v)
                    dst, scale = vt[:, t, tg(g)], 1.0
                else:
                    dst = ((q_a, k_a) if c < 9 else (q_b, k_b))[kind][:, 2 * j + t, tg(g)]
                    scale = SCALE if kind == 0 else 1.0
                act.activation(dst, out_of(b), ACT.Copy, scale=scale).then_inc(read[b], 1)

            def spread_q(dst, src, tiles, r):
                act.wait_ge(read[3], r)
                for half in range(2):
                    rows = slice(64 * half, 64 * half + 64)
                    for i in range(tiles):
                        hd = 2 * (i % 2 if tiles == 6 else i) + half
                        act.activation(dst[rows, i, :, hd], src[rows, i, SEQ:T], ACT.Copy).then_inc(qz_made, 1)

            for c in range(9):
                for b in range(4):
                    project_out(c, b)
                if c == 3:
                    act.wait_ge(pool_own, 2)
                    spread_q(qz_a, q_a, 6, R_QKV + 3)
                hi(QKV + c + 2)

            def a_where(u):
                r, hd = divmod(u, AH)
                return r, hd // 2, 64 * (hd % 2)

            def a_expo(u):
                act.wait_ge(a_max, u + 1)
                act.activation(sc[:, u % 2, :], sc[:, u % 2, :], ACT.Exp, bias=stat[:, 2 + u % 2:3 + u % 2],
                               accum_out=stat[:, 4 + u % 2:5 + u % 2]).then_inc(a_exp, 1)

            def a_top(u):
                r, t, po = a_where(u)
                act.wait_ge(a_out, u + 1)
                act.activation(oa_hi[po:po + 64, t, r:SEQ:4], ob[po:po + 64, 0:P], ACT.Copy).then_inc(a_hi, 1)

            a_expo(0)
            for u in range(16):
                if u >= 2:
                    a_top(u - 2)
                if u + 1 < 16:
                    a_expo(u + 1)
                for j in m2_pieces(u):
                    project_out(9 + j // 4, j % 4)
                act.wait_ge(a_turned, u + 1)
                if u >= 2:
                    act.wait_ge(a_out, u - 1)
                act.activation(p_t[:, u % 2, 0:512], tb[:], ACT.Copy).then_inc(a_pt_act, 1)
                for j in m2_pieces(u):
                    if j % 4 == 3:
                        hi(QKV + 9 + j // 4 + 2)
                if u == 8:
                    spread_q(qz_b, q_b, 4, R_QKV + 11)
            a_top(14)
            a_top(15)

            def b_sigmoid(w):
                hd, i = divmod(w, NB)
                act.wait_ge(b_scored, w + 1)
                if w >= 2:
                    act.wait_ge(b_turned, w - 1)
                n = (i + 1) * P
                act.activation(beta[:, w % 2, 0:n], (s1, s2)[w % 2][:, 0:n], ACT.Sigmoid,
                               bias=bias_b[:, hd:hd + 1]).then_inc(b_beta, 1)

            def b_top(w):
                hd, i = divmod(w, NB)
                po = 64 * (hd % 2)
                act.wait_ge(b_out, w + 1)
                act.activation(ob_hi[po:po + 64, hd // 2, i * P:(i + 1) * P], ob[po:po + 64, 0:P],
                               ACT.Copy).then_inc(b_hi, 1)

            def gate_out(dst, r0, j):
                c, b = divmod(j, 4)
                act.wait_ge(full[b], r0 + c + 1)
                act.activation(dst[:, 2 * c + b % 2, tg(b // 2)], out_of(b), ACT.Sigmoid).then_inc(read[b], 1)

            b_sigmoid(0)
            act.wait_ge(ka_out, 48)
            act.wait_ge(va_out, 48)
            for w in range(32):
                if w >= 2:
                    b_top(w - 2)
                if w + 1 < 32:
                    b_sigmoid(w + 1)
                if w % 2 == 1:
                    gate_out(gate_a, R_GA, w // 2)
                act.wait_ge(b_turned, w + 1)
                if w >= 2:
                    act.wait_ge(b_out, w - 1)
                n = (w % NB + 1) * P
                act.activation(w_t[:, w % 2, 0:n], tb[:, 0:n], ACT.Copy).then_inc(b_wt, 1)
                if w % 8 == 7:
                    hi(GA + w // 8 + 2)
            b_top(30)
            b_top(31)
            act.wait_ge(kb_out, 32)
            act.wait_ge(vb_out, 32)
            def fold_copy(x, src):
                act.activation(folded[x], src[:], ACT.Copy).then_inc(fold_copied, 1)

            def fold_top(x, src, dst, n):
                act.wait_ge(fold_turned, x + 1)
                for half in range(2):
                    rows = slice(64 * half, 64 * half + 64)
                    act.activation(dst[rows], fold_view(src, n)[rows, :, :, :, half], ACT.Copy).then_inc(s_hi, 1)

            for j in range(16):
                gate_out(gate_b, R_GB, j)
                if j == 2:
                    act.wait_ge(s_max, 1)
                    for r in range(2):
                        act.activation(s_a[:, r, :], s_a[:, r, :], ACT.Exp, bias=stat[:, 10 + r:11 + r],
                                       accum_out=stat[:, 12 + r:13 + r]).then_inc(s_exp, 1)
                if j == 5:
                    act.wait_ge(s_turned, 1)
                    turned = tb[:].rearrange("p (r n c) -> p r n c", r=2, n=2)
                    dst = pt_a.rearrange("p (r n) c -> p r n c", r=2)
                    act.activation(dst[:, :, 0, :], turned[:, :, 0, :], ACT.Copy).then_inc(s_pt, 1)
                    act.activation(dst[0:83, :, 1, :], turned[0:83, :, 1, :], ACT.Copy).then_inc(s_pt, 1)
                if j == 7:
                    act.wait_ge(ring_used, 24)
                    act.activation(s_beta.rearrange("p r k -> p (r k)"), s2[:], ACT.Sigmoid,
                                   bias=bias_b[:, BH:BH + 1]).then_inc(s_sig, 1)
                if j == 9:
                    act.wait_ge(s_turned, 2)
                    act.activation(pt_b.rearrange("p n c -> p (n c)"), ob[:], ACT.Copy).then_inc(s_pt, 1)
                    act.wait_ge(s_prob, 3)
                    fold_copy(0, s1)
                if j == 12:
                    fold_top(0, tb, sample_columns(oa_hi), 2)
                if j == 13:
                    act.wait_ge(sb_out, 1)
                    fold_copy(1, s2)
                if j % 4 == 3:
                    hi(GB + j // 4 + 2)
            act.wait_ge(sb_out, 2)
            fold_copy(2, ob)
            for x in range(2):
                fold_top(1 + x, (s1, s2)[x], sample_columns(ob_hi, x), 4)
            hi(PA + 2)

            def m_round(x):
                act.wait_ge(m_sum, x + 1)
                r, b = divmod(x, 4)
                act.activation(m_hi[:, 2 * r + b % 2, tg(b // 2)], m_tmp[x % 4], ACT.Copy).then_inc(m_top, 1)

            for x in range(16):
                m_round(x)
                if x % 8 == 7:
                    hi(PB + x // 8 + 2)
            outputs(1, R_WO, WO, 1)
            ffn_up(FFN2, R_FFN2)
            outputs(2, R_FFN2 + 2 * UPS, FFN2 + 2 * UPS, KC)

        @block.vector
        def _(dve):
            def drain():
                dve.drain()

            def u_of(q, g):
                dve.wait_ge(root_made, pre_root(q, g))
                drain()
                dve.reciprocal(rinv[:, g, :], root[:, g, :])
                drain()
                r = rinv[:, g:g + 1, :].to_broadcast([P, 2, TG])
                for s in range(4):
                    part = slice(2 * s, 2 * s + 2)
                    dve.tensor_tensor(f[:, part, tg(g)], h[:, part, tg(g)], r, ALU.mult).then_inc(hn_made, 1)
                drain()
                for t in range(KD):
                    dve.wait_ge(uh_made, 16 * q + 8 * g + t + 1)
                    dve.scalar_tensor_tensor(u_lo[:, t, tg(g)], f[:, t, tg(g)], gain[:, 2 * q, t:t + 1],
                                             u_hi[:, t, tg(g)].bitcast(F32), ALU.mult,
                                             ALU.subtract).then_inc(u_made, 1)

            def h_of(p, g):
                dve.wait_ge(root_made, post_root(p, g))
                drain()
                dve.reciprocal(rinv[:, g, :], root[:, g, :])
                drain()
                r = rinv[:, g:g + 1, :].to_broadcast([P, 2, TG])

                def scale(s):
                    part = f[:, 2 * s:2 * s + 2, tg(g)]
                    dve.tensor_tensor(part, part, r, ALU.mult)

                def add(s):
                    part = h[:, 2 * s:2 * s + 2, tg(g)]
                    dve.tensor_tensor(part, part, f[:, 2 * s:2 * s + 2, tg(g)], ALU.add).then_inc(h_ready, 1)

                scale(0)
                scale(1)
                for s in range(4):
                    drain()
                    add(s)
                    if s < 2:
                        scale(s + 2)

            def take_out(p, r0, r, b):
                g, t = divmod(b, 2)
                dve.wait_ge(post_sq, 4 * (4 * p + r) + b + 1)
                dve.tensor_scalar(f[:, 2 * r + t, tg(g)], out_of(b), gain[:, 2 * p + 1, 2 * r + t:2 * r + t + 1],
                                  None, ALU.mult).then_inc(read[b], 1)
                if r == 0 and t == 0:
                    dve.tensor_copy(acc[:, g, :], sqa[:, b, :]).then_inc(acc_added, 1)
                else:
                    dve.tensor_tensor(acc[:, g, :], acc[:, g, :], sqa[:, b, :], ALU.add).then_inc(acc_added, 1)
                drain()

            def outputs(p, r0):
                for r in range(DNS):
                    for b in range(4):
                        take_out(p, r0, r, b)
                        if r == DNS - 1 and b == 1:
                            h_of(p, 0)
                if p < 2:
                    u_of(p + 1, 0)
                h_of(p, 1)
                if p < 2:
                    u_of(p + 1, 1)

            def ffn_up(r0):
                with dve.Fori(0, UPS) as i:
                    for b in range(4):
                        g, t = divmod(b, 2)
                        dve.wait_ge(full[b], r0 + 2 + 2 * i)
                        x = tmp[:, b % 2, :]
                        dve.tensor_tensor(x, sg[:, b, :], out_of(b), ALU.mult).then_inc(read[b], 1)
                        drain()
                        top = hid_hi[:, bass.ds(2 * i + t, 1), tg(g)].rearrange("p a c -> p (a c)")
                        dve.tensor_copy(top, x)
                        drain()
                        low = hid_lo[:, bass.ds(2 * i + t, 1), tg(g)].rearrange("p a c -> p (a c)")
                        dve.tensor_tensor(low, x, top.bitcast(F32), ALU.subtract).then_inc(hid_made, 1)

            dve.memset(eps[:], EPS).then_inc(consts_ready, 1)
            dve.wait_ge(const_in, 64)
            for site in (1, 5):
                dve.tensor_scalar(gain[:, site, :], gain[:, site, :], 0.5, None, ALU.mult).then_inc(consts_ready, 1)
            u_of(0, 0)
            u_of(0, 1)
            ffn_up(R_FFN1)
            outputs(0, R_FFN1 + 2 * UPS)

            def place_v(n):
                dst = v_a[:, :, n * 256:(n + 1) * 256] if n < 3 else v_b[:, :, (n - 3) * 256:(n - 2) * 256]
                c = 3 * n if n < 4 else 11
                for t in range(2):
                    dve.wait_ge(v_turned, c + t + 1)
                    dve.tensor_copy(dst[:, :, t * P:(t + 1) * P],
                                    (tb, ob)[t][:].rearrange("p (k c) -> p k c", k=NB)).then_inc(v_placed, 1)
                if n < 3:
                    dve.wait_ge(v_turned, c + 3)
                    dve.tensor_copy(v_self[:, n * 256:(n + 1) * 256], tb[0:DEC, 0:256]).then_inc(v_placed, 1)

            place_v(0)
            place_v(1)
            dve.wait_ge(mix_in, 64)

            def a_bias(u):
                r, hd = divmod(u, AH)
                x = sc[:, u % 2, :]
                dve.wait_ge(a_scored, u + 1)
                if u >= 2:
                    dve.wait_ge(a_turned, u - 1)
                for g, (dst, src, dist) in enumerate(((x[:, 0:512], s1[:], dist1[:, 3 - r:515 - r]),
                                                      (x[:, 512:640], s2[:, 0:P], dist2[:]),
                                                      (x[:, 640:768], s2[:, P:2 * P], dist3[:]))):
                    dve.scalar_tensor_tensor(dst, dist, -slope(g, hd), src, ALU.mult, ALU.add).then_inc(a_biased, 1)
                drain()
                dve.tensor_reduce(stat[:, u % 2:u % 2 + 1], x, AX.X, ALU.max)
                drain()
                dve.tensor_scalar(stat[:, 2 + u % 2:3 + u % 2], stat[:, u % 2:u % 2 + 1], -1.0, None,
                                  ALU.mult).then_inc(a_max, 1)

            def a_norm(u):
                dve.wait_ge(a_exp, u + 1)
                dve.reciprocal(stat[:, 6 + u % 2:7 + u % 2], stat[:, 4 + u % 2:5 + u % 2])
                drain()
                dve.tensor_scalar(sc[:, u % 2, :], sc[:, u % 2, :], stat[:, 6 + u % 2:7 + u % 2], None,
                                  ALU.mult).then_inc(a_prob, 1)

            def a_low(u):
                r, hd = divmod(u, AH)
                t, po = hd // 2, 64 * (hd % 2)
                dve.wait_ge(a_hi, u + 1)
                dve.tensor_tensor(oa_lo[po:po + 64, t, r:SEQ:4], ob[po:po + 64, 0:P],
                                  oa_hi[po:po + 64, t, r:SEQ:4].bitcast(F32), ALU.subtract).then_inc(a_lo, 1)

            a_bias(0)
            for u in range(16):
                if u == 0:
                    place_v(2)
                a_norm(u)
                if u >= 2:
                    a_low(u - 2)
                if u + 1 < 16:
                    a_bias(u + 1)
                if u == 13:
                    place_v(3)
                dve.wait_ge(a_turned, u + 1)
                if u >= 2:
                    dve.wait_ge(a_out, u - 1)
                dve.tensor_copy(p_t[:, u % 2, 512:768], s2[:, 256:512]).then_inc(a_pt_dve, 1)
            a_low(14)
            a_low(15)

            def b_chain(w):
                i = w % NB
                n = (i + 1) * P
                x = beta[:, w % 2, 0:n]
                dve.wait_ge(b_beta, w + 1)
                dve.tensor_tensor(x[:, n - P:n], x[:, n - P:n], tri[:], ALU.mult)
                drain()
                dve.tensor_scalar(keep[:, 0:n], x, -1.0, 1.0, ALU.mult, ALU.add)
                drain()
                dve.tensor_tensor_scan(suffix[:, 512 - n:512][:, ::-1], keep[:, 0:n][:, ::-1], keep[:, 0:n], 1.0,
                                       ALU.mult, ALU.bypass)
                drain()
                dve.tensor_tensor(x, x, suffix[:, 513 - n:513], ALU.mult).then_inc(b_weight, 1)

            def b_low(w):
                hd, i = divmod(w, NB)
                po = 64 * (hd % 2)
                dve.wait_ge(b_hi, w + 1)
                dst = slice(i * P, (i + 1) * P)
                dve.tensor_tensor(ob_lo[po:po + 64, hd // 2, dst], ob[po:po + 64, 0:P],
                                  ob_hi[po:po + 64, hd // 2, dst].bitcast(F32), ALU.subtract).then_inc(b_lo, 1)

            dve.wait_ge(b_scored, 1)
            dve.memset(suffix[:, 512:513], 1.0)
            b_chain(0)
            for w in range(32):
                if w >= 2:
                    b_low(w - 2)
                if w == 1:
                    place_v(4)
                if w + 1 < 32:
                    b_chain(w + 1)
            b_low(30)
            b_low(31)

            dve.wait_ge(b_beta, 32)
            for score in (s1, s2):
                dve.memset(score[:], 0.0).then_inc(s_zero, 1)
            dve.memset(s_suffix[:, :, 256:257], 1.0)
            dve.wait_ge(s_bias, 16)
            dve.wait_ge(ring_used, 8)
            dve.tensor_tensor(s_a[:], s_a[:], s1[:, 0:422].rearrange("p (r k) -> p r k", r=2), ALU.add)
            drain()
            dve.tensor_reduce(stat[:, 8:10], s_a[:], AX.X, ALU.max)
            drain()
            dve.tensor_scalar(stat[:, 10:12], stat[:, 8:10], -1.0, None, ALU.mult).then_inc(s_max, 1)
            dve.wait_ge(s_exp, 2)
            dve.reciprocal(stat[:, 14:16], stat[:, 12:14])
            drain()
            for r in range(2):
                dve.tensor_scalar(s_a[:, r, :], s_a[:, r, :], stat[:, 14 + r:15 + r], None,
                                  ALU.mult).then_inc(s_prob, 1)
            dve.wait_ge(s_sig, 1)
            dve.tensor_scalar(s_keep, s_beta, -1.0, 1.0, ALU.mult, ALU.add)
            drain()
            for r in range(2):
                dve.tensor_tensor_scan(s_suffix[:, r, 0:256][:, ::-1], s_keep[:, r, :][:, ::-1], s_keep[:, r, :],
                                       1.0, ALU.mult, ALU.bypass)
            drain()
            dve.tensor_tensor(s_beta, s_beta, s_suffix[:, :, 1:257], ALU.mult).then_inc(s_prob, 1)

            def fold_low(k, src, hi_t, lo_t, n, r=None):
                for half in range(2):
                    rows = slice(64 * half, 64 * half + 64)
                    dve.wait_ge(s_hi, k + half + 1)
                    dve.tensor_tensor(sample_columns(lo_t, r)[rows], fold_view(src, n)[rows, :, :, :, half],
                                      sample_columns(hi_t, r)[rows].bitcast(F32), ALU.subtract).then_inc(s_lo, 1)

            fold_low(0, tb, oa_hi, oa_lo, 2)
            for r in range(2):
                fold_low(2 + 2 * r, (s1, s2)[r], ob_hi, ob_lo, 4, r)

            for x in range(16):
                r, b = divmod(x, 4)
                g, t = divmod(b, 2)
                part = gate_a[:, 2 * r + t, tg(g)]
                dve.wait_ge(full[b], R_PA + r + 1)
                dve.tensor_tensor(part, part, out_of(b), ALU.mult).then_inc(read[b], 1)
            drain()

            def m_low(x):
                r, b = divmod(x, 4)
                where = (slice(None), 2 * r + b % 2, tg(b // 2))
                dve.wait_ge(m_top, x + 1)
                dve.tensor_tensor(m_lo[where], m_tmp[x % 4], m_hi[where].bitcast(F32),
                                  ALU.subtract).then_inc(m_made, 1)

            for x in range(16):
                r, b = divmod(x, 4)
                where = (slice(None), 2 * r + b % 2, tg(b // 2))
                dve.wait_ge(full[b], R_PB + r + 1)
                dve.tensor_tensor(m_tmp[x % 4], gate_b[where], out_of(b), ALU.mult).then_inc(read[b], 1)
                drain()
                dve.tensor_tensor(m_tmp[x % 4], m_tmp[x % 4], gate_a[where], ALU.add).then_inc(m_sum, 1)
                if x:
                    m_low(x - 1)
            m_low(15)
            outputs(1, R_WO)
            ffn_up(R_FFN2)
            outputs(2, R_FFN2 + 2 * UPS)

        @block.tensor
        def _(pe):
            def product(b, slot, kw, k, cols, x_hi, x_lo, kx, first, last):
                g = b // 2
                w = w_hi[:, slot, :].rearrange("p (k c) -> p k c", k=kw)[:, k, cols]
                v = w_lo[:, slot, :].rearrange("p (k c) -> p k c", k=kw)[:, k, cols]
                hi_x, lo_x = x_hi[:, kx, tg(g)], x_lo[:, kx, tg(g)]
                pe.matmul(out_of(b), w, hi_x, start=first, stop=False)
                pe.matmul(out_of(b), w, lo_x, start=False, stop=False)
                return pe.matmul(out_of(b), v, hi_x, start=False, stop=last)

            def tile_cols(b):
                t = b % 2
                return slice(t * P, (t + 1) * P)

            def u_item(slot, b, r, q=None, part=None):
                if part != 1:
                    pe.wait_ge(read[b], r)
                for k in {None: range(KD), 0: range(KD // 2), 1: range(KD // 2, KD)}[part]:
                    if q is not None and b % 2 == 0:
                        pe.wait_ge(u_made, 16 * q + 8 * (b // 2) + k + 1)
                    mm = product(b, slot, KD, k, tile_cols(b), u_hi, u_lo, k, k == 0, k == KD - 1)
                if part != 0:
                    mm.then_inc(full[b], 1)

            def sum_h(q, g):
                for t in range(KD):
                    pe.wait_ge(h_sq, 16 * q + 8 * g + t + 1)
                    pe.matmul(sum_pre[g][:, 0:TG], ones, sqb[:, t % 2, :], start=t == 0,
                              stop=t == KD - 1).then_inc(h_summed, 1)

            def sum_out(p, g):
                pe.wait_ge(acc_added, 4 * (4 * p + 3) + 2 * g + 2)
                pe.matmul(sum_post[g][:, 0:TG], ones, acc[:, g, :], start=True, stop=True).then_inc(post_summed, 1)

            def first_chunk(q, n, r):
                pe.wait_ge(lo_made, n + 1)
                for b in range(4):
                    u_item(n % 2, b, r, q)
                    if b == 1:
                        sum_h(q, 1)

            def ffn_up(q, n0, r0):
                first_chunk(q, n0, r0)
                pe.wait_ge(lo_made, n0 + 2)
                for b in range(4):
                    u_item(1, b, r0 + 1)
                with pe.Fori(1, UPS) as i:
                    for s in range(2):
                        pe.wait_ge(lo_made, n0 + 1 + s + 2 * i)
                        for b in range(4):
                            u_item(s, b, r0 + s + 2 * i)

            def down_chunk(p, slot, n, r, kc, i, last=False):
                pe.wait_ge(lo_made, n + 1)
                ks = min(KD, KF - KD * kc)
                made = 4 * UPS * (0 if p == 0 else 1)
                pe.wait_ge(hid_made, made + min(2 * KD * (kc + 1), 4 * UPS))
                for b in range(4):
                    if kc == 0:
                        pe.wait_ge(read[b], r)
                    for k in range(ks):
                        mm = product(b, slot, KD, k, tile_cols(b), hid_hi, hid_lo, KD * kc + k,
                                     kc == 0 and k == 0, kc == KC - 1 and k == ks - 1)
                    if kc == KC - 1:
                        mm.then_inc(full[b], 1)
                    elif b == 3:
                        mm.then_inc(part_used, 1)
                    if last and b == 2:
                        sum_out(p, 0)

            def boundary(p):
                if p < 2:
                    sum_h(p + 1, 0)
                sum_out(p, 1)

            def ffn_down(p, n0, r0):
                with pe.Fori(0, DNS // 2 - 1) as i:
                    for j in range(2 * KC):
                        down_chunk(p, j % 2, n0 + j + 2 * KC * i, r0 + j // KC + 2 * i, j % KC, i)
                n1, r1 = n0 + 2 * KC * (DNS // 2 - 1), r0 + DNS - 2
                for j in range(2 * KC):
                    down_chunk(p, j % 2, n1 + j, r1 + j // KC, j % KC, 0, last=j == 2 * KC - 1)
                boundary(p)

            pe.wait_ge(const_in, 64)
            sum_h(0, 0)
            ffn_up(0, FFN1, R_FFN1)
            ffn_down(0, FFN1 + 2 * UPS, R_FFN1 + 2 * UPS)

            def turn_v(n):
                r = R_QKV + (6 + n if n < 3 else 10 + n)
                pe.wait_ge(read[3], r + 1)
                for t in range(2):
                    if n == 4:
                        pe.wait_ge((a_pt_act, a_lo)[t], 16)
                    elif n == 3:
                        pe.wait_ge((a_pt_act, a_lo)[t], 13 - t)
                    elif n:
                        pe.wait_ge(v_placed, 3 * n)
                    for blk in range(NB):
                        src = vt[:, t, blk:SEQ:4] if n in (1, 2) else vt[:, t, blk * P:(blk + 1) * P]
                        mm = pe.transpose((tb, ob)[t][:, blk * P:(blk + 1) * P], src, ident)
                    mm.then_inc(v_turned, 1)
                if n < 3:
                    pe.wait_ge(v_placed, 3 * n + 1)
                    for t in range(2):
                        mm = pe.transpose(tb[0:DEC, t * P:(t + 1) * P], vt[:, t, SEQ:T], ident)
                    mm.then_inc(v_turned, 1)

            first_chunk(1, QKV, R_QKV)
            for c in range(1, 9):
                pe.wait_ge(lo_made, QKV + c + 1)
                for b in range(4):
                    u_item((QKV + c) % 2, b, R_QKV + c)
                    if b == 0 and c > 6:
                        turn_v(c - 7)

            def a_scores(u):
                r, hd = divmod(u, AH)
                t, po = hd // 2, 64 * (hd % 2)
                rows = slice(po, po + 64)
                if u:
                    pe.wait_ge(a_biased, 3 * u)
                    pe.wait_ge(a_pt_dve, u - 1)
                pe.matmul(s1[:], q_a[rows, t, r:SEQ:4], k_a[rows, t, 0:SEQ], start=True, stop=True)
                pe.matmul(s2[:, 0:P], q_a[rows, 2 + t, r:SEQ:4], k_a[rows, 2 + t, r:SEQ:4], start=True, stop=True)
                pe.matmul(s2[:, P:2 * P], q_a[rows, 4 + t, r:SEQ:4], k_a[rows, 4 + t, r:SEQ:4], start=True,
                          stop=True).then_inc(a_scored, 1)

            def a_turn(u):
                pe.wait_ge(a_prob, u + 1)
                pe.wait_ge(a_pt_act, u)
                pe.wait_ge(v_placed, 9 + 2 * (u >= 13))
                pe.wait_ge(a_biased, 3 * min(u + 2, 16))
                for n in range(6):
                    dst = tb[:, n * P:(n + 1) * P] if n < 4 else s2[:, (n - 2) * P:(n - 1) * P]
                    mm = pe.transpose(dst, sc[:, u % 2, n * P:(n + 1) * P], ident)
                mm.then_inc(a_turned, 1)

            def a_apply(u):
                r, hd = divmod(u, AH)
                po = 64 * (hd % 2)
                pe.wait_ge(a_pt_act, u + 1)
                pe.wait_ge(a_pt_dve, u + 1)
                pe.wait_ge(a_lo, u)
                for n in range(6):
                    g, blk = (0, n) if n < 4 else (n - 3, r)
                    col = g * 256 + hd * DH
                    mm = pe.matmul(ob[po:po + 64, 0:P], v_a[:, blk, col:col + DH], p_t[:, u % 2, n * P:(n + 1) * P],
                                   start=n == 0, stop=n == 5)
                mm.then_inc(a_out, 1)

            pe.wait_ge(read[3], R_QKV + 6)
            a_scores(0)
            for u in range(16):
                if u + 1 < 16:
                    a_scores(u + 1)
                for j in m2_pieces(u):
                    if j % 4 == 0:
                        pe.wait_ge(lo_made, QKV + 9 + j // 4 + 1)
                    u_item((QKV + 9 + j // 4) % 2, j % 4, R_QKV + 9 + j // 4)
                    if j == 0:
                        turn_v(2)
                    if j == 20:
                        turn_v(3)
                a_turn(u)
                if u:
                    a_apply(u - 1)
            a_apply(15)

            def b_scores(w):
                hd, i = divmod(w, NB)
                t, po = hd // 2, 64 * (hd % 2)
                n = (i + 1) * P
                if w < 2:
                    pe.wait_ge((a_biased, a_pt_dve)[w], (48, 16)[w])
                else:
                    pe.wait_ge(b_beta, w - 1)
                pe.matmul((s1, s2)[w % 2][:, 0:n], q_b[po:po + 64, t, i * P:n], k_b[po:po + 64, t, 0:n],
                          start=True, stop=True).then_inc(b_scored, 1)

            def b_turn(w):
                pe.wait_ge(b_weight, w + 1)
                pe.wait_ge(b_wt, w)
                for n in range(w % NB + 1):
                    mm = pe.transpose(tb[:, n * P:(n + 1) * P], beta[:, w % 2, n * P:(n + 1) * P], ident)
                mm.then_inc(b_turned, 1)

            def b_apply(w):
                hd, i = divmod(w, NB)
                po = 64 * (hd % 2)
                pe.wait_ge(b_wt, w + 1)
                pe.wait_ge(b_lo, w)
                for n in range(i + 1):
                    mm = pe.matmul(ob[po:po + 64, 0:P], v_b[:, n, hd * DH:(hd + 1) * DH],
                                   w_t[:, w % 2, n * P:(n + 1) * P], start=n == 0, stop=n == i)
                mm.then_inc(b_out, 1)

            b_scores(0)
            for w in range(32):
                if w + 1 < 32:
                    b_scores(w + 1)
                j = w // 2
                if w % 8 == 0:
                    pe.wait_ge(lo_made, GA + j // 4 + 1)
                u_item((GA + j // 4) % 2, j % 4, R_GA + j // 4, part=w % 2)
                if w == 0:
                    turn_v(4)
                    pe.wait_ge(v_placed, 13)
                b_turn(w)
                if w:
                    b_apply(w - 1)
            b_apply(31)

            def sample_keys(x):
                pe.wait_ge(ring_in[x % 4], 16 * (x // 4 + 1))
                slot = ring[x % 4]
                if x < DEC:
                    pe.wait_ge(self_in, 3 * (x + 1))
                    row, rnd = 32 * (x % 4), x // 4
                    for g, (k0, k1) in enumerate(((0, 129), (129, 194), (194, 211))):
                        for t in range(2):
                            mm = pe.matmul(s1[row:row + AH, rnd * 211 + k0:rnd * 211 + k1], qz_a[:, 2 * g + t, x, :],
                                           slot[:, t * 211 + k0:t * 211 + k1], start=t == 0, stop=t == 1)
                else:
                    b, pgi = divmod(x - DEC, 2)
                    row, col = 32 * (b % 4), (b // 4) * 256 + pgi * P
                    for t in range(4):
                        mm = pe.matmul(s2[row:row + BH, col:col + P], qz_b[:, t, b, :], slot[:, t * P:(t + 1) * P],
                                       start=t == 0, stop=t == 3)
                mm.then_inc(ring_used, 1)

            def sample_turn_a():
                pe.wait_ge(s_prob, 2)
                pe.wait_ge(b_wt, 32)
                for r in range(2):
                    pe.transpose(tb[:, 2 * r * P:(2 * r + 1) * P], s_a[:, r, 0:P], ident)
                    mm = pe.transpose(tb[0:83, (2 * r + 1) * P:(2 * r + 2) * P], s_a[:, r, P:211], ident)
                mm.then_inc(s_turned, 1)

            def sample_turn_b():
                pe.wait_ge(s_prob, 3)
                pe.wait_ge(b_lo, 32)
                for n in range(4):
                    r, pgi = divmod(n, 2)
                    mm = pe.transpose(ob[:, n * P:(n + 1) * P], s_beta[:, r, pgi * P:(pgi + 1) * P], ident)
                mm.then_inc(s_turned, 1)

            def sample_values_a(b):
                row, rnd = 32 * (b % 4), b // 4
                for t in range(2):
                    cols = slice(row + 2 * t, row + 2 * t + 2)
                    out = s1[row:row + 2, (2 * t + rnd) * P:(2 * t + rnd + 1) * P]
                    pe.matmul(out, pt_a[:, 2 * rnd, cols], va_1[:, b, t * P:(t + 1) * P], start=True, stop=False)
                    mm = pe.matmul(out, pt_a[0:83, 2 * rnd + 1, cols], va_23[:, b, t * P:(t + 1) * P],
                                   start=False, stop=True)
                if b == DEC - 1:
                    mm.then_inc(va_used, 1)

            def sample_values_b(b):
                row, rnd = 32 * (b % 4), b // 4
                for n in range(2):
                    x = 2 * b + n
                    if x < 4:
                        pe.wait_ge(ring_in[x], 16 * 7)
                    elif x < 12:
                        pe.wait_ge(page_in[x - 4], 16)
                    else:
                        pe.wait_ge(ring_in[x - 12], 16 * 8)
                for t in range(4):
                    cols = slice(row + 2 * t, row + 2 * t + 2)
                    for n in range(2):
                        mm = pe.matmul((s2, ob)[rnd][row:row + 2, t * P:(t + 1) * P], pt_b[:, 2 * rnd + n, cols],
                                       blocks[(2 * b + n) % 12][:, t * P:(t + 1) * P], start=n == 0, stop=n == 1)
                        if b < 2 and t == 3:
                            mm.then_inc(ring_used, 1)
                if b % 4 == 3:
                    mm.then_inc(sb_out, 1)

            def fold_turn(x, dst):
                pe.wait_ge(fold_copied, x + 1)
                for n in range(4):
                    mm = pe.transpose(dst[:, n * P:(n + 1) * P], folded[x][:, n * P:(n + 1) * P], ident)
                mm.then_inc(fold_turned, 1)

            pe.wait_ge(s_zero, 2)
            pe.wait_ge(qz_made, 20)
            key_units = (4, 4, 3, 3, 3, 3, 2, 2)
            x = 0
            for j in range(16):
                if j % 4 == 0:
                    pe.wait_ge(lo_made, GB + j // 4 + 1)
                u_item((GB + j // 4) % 2, j % 4, R_GB + j // 4)
                if j < 8:
                    for _ in range(key_units[j]):
                        sample_keys(x)
                        x += 1
                if j == 4:
                    sample_turn_a()
                if j in (6, 7):
                    if j == 6:
                        pe.wait_ge(s_pt, 2)
                        pe.wait_ge(va_in, 96)
                    for b in range(4 * (j - 6), 4 * (j - 6) + 4):
                        sample_values_a(b)
                if j == 9:
                    sample_turn_b()
                if j == 10:
                    fold_turn(0, tb)
                    pe.wait_ge(s_pt, 3)
                if 11 <= j < 15:
                    for b in range(2 * (j - 11), 2 * (j - 11) + 2):
                        sample_values_b(b)
                if j == 15:
                    fold_turn(1, s1)

            pe.wait_ge(s_lo, 2)
            pe.wait_ge(lo_made, PA + 1)
            for x in range(16):
                r, b = divmod(x, 4)
                col = (2 * r + b % 2) * P
                if x == 2:
                    fold_turn(2, s2)
                pe.wait_ge(read[b], R_PA + r)
                for k in range(2):
                    mm = product(b, PA % 2, 2, k, slice(col, col + P), oa_hi, oa_lo, k, k == 0, k == 1)
                mm.then_inc(full[b], 1)
            for x in range(16):
                r, b = divmod(x, 4)
                n, col = PB + r // 2, (2 * (r % 2) + b % 2) * P
                if x == 0:
                    pe.wait_ge(s_lo, 6)
                if x % 8 == 0:
                    pe.wait_ge(lo_made, n + 1)
                pe.wait_ge(read[b], R_PB + r)
                for k in range(4):
                    mm = product(b, n % 2, 4, k, slice(col, col + P), ob_hi, ob_lo, k, k == 0, k == 3)
                mm.then_inc(full[b], 1)
            pe.wait_ge(m_made, 16)
            for r in range(DNS):
                n = WO + r
                pe.wait_ge(lo_made, n + 1)
                for b in range(4):
                    pe.wait_ge(read[b], R_WO + r)
                    for k in range(KD):
                        mm = product(b, n % 2, KD, k, tile_cols(b), m_hi, m_lo, k, k == 0, k == KD - 1)
                    mm.then_inc(full[b], 1)
                    if r == DNS - 1 and b == 2:
                        sum_out(1, 0)
            boundary(1)
            ffn_up(2, FFN2, R_FFN2)
            ffn_down(2, FFN2 + 2 * UPS, R_FFN2 + 2 * UPS)


def _chunk(w, rows, cols):
    import numpy as np
    k = (rows.stop - rows.start) // P
    c = w[rows, cols].reshape(k, P, cols.stop - cols.start).transpose(1, 0, 2).reshape(P, -1)
    if c.shape[1] < CH:
        c = np.concatenate([c, np.zeros((P, CH - c.shape[1]), c.dtype)], axis=1)
    return c


def _stream(gate, up, down, w_in, p_a, p_b, w_o, gate2, up2, down2):
    import numpy as np
    every = slice(0, D)

    def ffn(wg, wu, wd):
        for j in range(UPS):
            for w in (wg, wu):
                yield _chunk(w, every, slice(j * CW, (j + 1) * CW))
        for j in range(DNS):
            for kc in range(KC):
                yield _chunk(wd, slice(kc * D, min((kc + 1) * D, FF)), slice(j * CW, (j + 1) * CW))

    chunks = list(ffn(gate, up, down))
    chunks += [_chunk(w_in, every, slice(j * CW, (j + 1) * CW)) for j in range(w_in.shape[1] // CW)]
    chunks.append(_chunk(p_a, slice(0, 256), every))
    chunks += [_chunk(p_b, slice(0, WB), slice(j * 512, (j + 1) * 512)) for j in range(2)]
    chunks += [_chunk(w_o, every, slice(j * CW, (j + 1) * CW)) for j in range(DNS)]
    chunks += list(ffn(gate2, up2, down2))
    return np.stack(chunks)


def _tables():
    import numpy as np
    a = np.arange(P)[:, None]
    d1 = 4 * a - (np.arange(515)[None, :] - 3)
    d1 = np.where((d1 >= 0) & (d1 <= P), d1, FAR)
    d = 4 * (a - np.arange(P)[None, :])
    d2 = np.where(d >= 0, d, FAR)
    d3 = np.where((d >= 0) & (d % 16 == 0), d, FAR)
    tri = (np.arange(P)[None, :] < a).astype(np.float64)
    consts = np.concatenate([np.eye(P), np.ones((P, P)), d1, d2, d3, tri], axis=1).astype(np.float32)
    dist = [128.0 - np.arange(128), [0.0], 256.0 - 4.0 * np.arange(64), [0.0], 256.0 - 16.0 * np.arange(16), [0.0]]
    group = np.repeat([0, 0, 1, 1, 2, 2], [len(x) for x in dist])
    dist = np.concatenate(dist)
    bias = np.zeros((P, 2, 211), np.float32)
    for j in range(4):
        for hd in range(AH):
            bias[32 * j + hd] = [-slope(g, hd) * x for g, x in zip(group, dist)]
    return consts, bias.reshape(P, 422)


def kernel(x_prompt, x_sample, cache_a1_kv, cache_a2_kv, cache_a3_kv, cache_b_kv, page_table,
           g_ffn1_pre, g_ffn1_post, w1_gate, w1_up, w1_down, g_mix_pre, g_mix_post, w_in, b_sb,
           p_a, p_b, w_o, g_ffn2_pre, g_ffn2_post, w2_gate, w2_up, w2_down):
    import numpy as np
    import concourse.bacc as bacc
    from concourse.bass_utils import run_bass_kernel_spmd

    n = {k: np.asarray(v) for k, v in locals().items() if k not in ("np", "bacc", "run_bass_kernel_spmd")}
    x = np.concatenate([n["x_prompt"][0], n["x_sample"][:, 0]], axis=0)
    gains = np.stack([n[k][0] for k in ("g_ffn1_pre", "g_ffn1_post", "g_mix_pre", "g_mix_post", "g_ffn2_pre",
                                        "g_ffn2_post")])
    b_rows = n["b_sb"][0]
    consts, sample_bias = _tables()
    gap = np.zeros((DEC, 1, AH * DH), np.float32)
    rows = [c[0][:, ::s] for c, s in ((n["cache_a1_kv"], 1), (n["cache_a2_kv"], 4), (n["cache_a3_kv"], 16))]
    keys = [r[:, :, 0].reshape(DEC, -1, AH * DH) for r in rows]
    vals = [r[:, :, 1].reshape(DEC, -1, AH * DH) for r in rows]
    ka = np.concatenate([keys[0], gap, keys[1], gap, keys[2], gap], axis=1)
    ka = ka.reshape(DEC, 211, 2, P).transpose(0, 3, 2, 1).reshape(DEC, P, 422)
    pool = n["cache_b_kv"][0]
    n_phys = pool.shape[0]
    kb = pool[:, :, 0].reshape(n_phys, P, 4, P).transpose(0, 3, 2, 1).reshape(n_phys, P, 512)
    arrays = {
        "w_stream": _stream(*(n[k][0] for k in ("w1_gate", "w1_up", "w1_down", "w_in", "p_a", "p_b", "w_o",
                                                "w2_gate", "w2_up", "w2_down"))),
        "x_t": x.reshape(T, KD, P).transpose(2, 1, 0),
        "gains_in": gains.reshape(6, KD, P).transpose(2, 0, 1),
        "b_rows": np.concatenate([np.tile(b_rows, (P, 1)), np.tile(b_rows, P // BH)[:, None]], axis=1),
        "consts": consts,
        "sample_bias": sample_bias,
        "ka_cache": ka,
        "va_cache1": vals[0].transpose(1, 0, 2),
        "va_cache2": np.concatenate([vals[1], vals[2]], axis=1).transpose(1, 0, 2),
        "kb_pool": kb,
        "vb_pool": pool[:, :, 1].reshape(n_phys, P, 512),
        "pages": n["page_table"].reshape(1, -1),
    }
    outs = {
        "y_t": (P, KD, T), "ka1_t": (P, 2, P + DEC), "ka2_t": (P, 2, T), "ka3_t": (P, 2, T), "kb_t": (P, 4, T),
        "va1_o": (P, 256), "va2_o": (P, NB, 256), "va3_o": (P, NB, 256), "vb_o": (P, NB, 512), "vs_t": (P, 10, DEC),
    }
    nc = bacc.Bacc("TRN2", target_bir_lowering=False, num_devices=1)
    arrays = {k: np.ascontiguousarray(v) for k, v in arrays.items()}
    args = [nc.dram_tensor(k, a.shape, mybir.dt.from_np(a.dtype), kind="ExternalInput").ap() for k, a in arrays.items()]
    args += [nc.dram_tensor(k, s, F32, kind="ExternalOutput").ap() for k, s in outs.items()]
    step_program(nc, *args)
    o = run_bass_kernel_spmd(nc, [arrays], core_ids=[0]).results[0]
    o = {k: np.asarray(o[k]) for k in outs}

    def rows_of(t):
        return t.transpose(2, 1, 0).reshape(t.shape[2], -1)

    y = rows_of(o["y_t"])
    result = [y[None, :SEQ], y[SEQ:, None]]
    vs = rows_of(o["vs_t"])
    values = [o["va1_o"], o["va2_o"].reshape(SEQ, 256), o["va3_o"].reshape(SEQ, 256)]
    for g in range(AG):
        k = rows_of(o[f"ka{g + 1}_t"])
        past = k.shape[0] - DEC
        both = np.stack([k[:past], values[g]], axis=1).reshape(1, 1, past, 2, AH, DH)
        new = np.stack([k[past:], vs[:, g * 256:(g + 1) * 256]], axis=1).reshape(1, DEC, 1, 2, AH, DH)
        result += [both, new]
    k = rows_of(o["kb_t"])
    v = o["vb_o"].transpose(1, 0, 2).reshape(SEQ, 512)
    result.append(np.stack([k[:SEQ], v], axis=1).reshape(1, 1, NB, P, 2, BH, DH))
    result.append(np.stack([k[SEQ:], vs[:, 768:]], axis=1).reshape(1, DEC, 1, 2, BH, DH))
    return tuple(result)
```

```python
from contextlib import ExitStack

import concourse.bass as bass
from concourse import mybir

F32 = mybir.dt.float32
F32R = mybir.dt.float32r
I32 = mybir.dt.int32
ALU = mybir.AluOpType
ACT = mybir.ActivationFunctionType
AX = mybir.AxisListType

P = 128
D = 1024
KD = D // P
SEQ = 512
NB = SEQ // P
DEC = 8
T = SEQ + DEC
G = 2
TG = T // G
FF = 2816
CW = 256
CH = KD * CW
UPS = FF // CW
KF = FF // P
DNS = D // CW
KC = -(-KF // KD)
DH = 64
AG, AH, BH = 3, 4, 8
WA, WB = AG * AH * DH, BH * DH
DIL = (1, 4, 16)
PAST = 256
EPS = 1e-6
SCALE = DH ** -0.5
FAR = 1e30

FFN1, QKV, GA, GB, PA, PB, WO, FFN2 = 0, 34, 49, 53, 57, 58, 60, 64
CHUNKS = 98
R_FFN1, R_QKV, R_GA, R_GB, R_PA, R_PB, R_WO, R_FFN2 = 0, 26, 41, 45, 49, 53, 57, 61


def slope(g, h):
    return 2.0 ** (-8.0 * (g * AH + h + 1) / (AG * AH))


class Placed:

    def __init__(self, nc, at):
        self.nc, self.at = nc, at

    def __call__(self, name, shape, dt=F32):
        n = 4
        for s in shape[1:]:
            n *= s
        t = self.nc.alloc_sbuf_tensor_at(name, shape, dt, offset=self.at)
        self.at += -(-n // 32) * 32
        return t


def step_program(nc, w_stream, x_t, gains_in, b_rows, consts, sample_bias, ka_cache, va_cache1,
                 va_cache2, kb_pool, vb_pool, pages, y_t, ka1_t, ka2_t, ka3_t, kb_t, va1_o, va2_o,
                 va3_o, vb_o, vs_t):
    base = -(-nc.sbuf_base // 32) * 32
    perm = Placed(nc, base)
    h = perm("h", [P, KD, T])
    w_hi = perm("w_hi", [P, 2, CH], F32R)
    w_lo = perm("w_lo", [P, 2, CH], F32R)
    raw = perm("raw", [P, 2, CH])
    u_hi = perm("u_hi", [P, KD, T], F32R)
    f = Placed(nc, perm.at)("f", [P, KD, T])
    u_lo = perm("u_lo", [P, KD, T], F32R)
    cst = perm("cst", [P, 2 * P])
    gain = perm("gain", [P, 6, KD])
    bias_b = perm("bias_b", [P, BH + 1])
    eps = perm("eps", [P, 1])
    stat = perm("stat", [P, 16])
    warm = perm("warm", [P, 1])
    tmp = perm("tmp", [P, 2, TG])
    sqa = perm("sqa", [P, 4, TG])
    sqb = perm("sqb", [P, 2, TG])
    acc = perm("acc", [P, G, TG])
    root = perm("root", [P, G, TG])
    rinv = perm("rinv", [P, G, TG])
    pg = perm("pg", [P, 2 * DEC], I32)
    ident, ones = cst[:, 0:P], cst[:, P:2 * P]
    R = perm.at
    ffn = Placed(nc, R)
    hid_hi = ffn("hid_hi", [P, KF, T], F32R)
    hid_lo = ffn("hid_lo", [P, KF, T], F32R)
    sg = ffn("sg", [P, 4, TG])
    mix = Placed(nc, R)
    oa_hi = mix("oa_hi", [P, 2, T], F32R)
    oa_lo = mix("oa_lo", [P, 2, T], F32R)
    q_a = mix("q_a", [P, 6, T])
    k_a = mix("k_a", [P, 6, T])
    v_a = mix("v_a", [P, NB, WA])
    vt = mix("vt", [P, 2, T])
    v_self = mix("v_self", [DEC, WA])
    k_self = mix("k_self", [P, 6, DEC])
    qz_a = mix("qz_a", [P, 6, DEC, AH])
    qz_b = mix("qz_b", [P, 4, DEC, BH])
    dist1 = mix("dist1", [P, 520])
    dist2 = mix("dist2", [P, P])
    dist3 = mix("dist3", [P, P])
    tri = mix("tri", [P, P])
    work = mix.at
    sc = mix("sc", [P, 2, 768])
    p_t = mix("p_t", [P, 2, 768])
    q_b = mix("q_b", [P, 4, T])
    k_b = mix("k_b", [P, 4, T])
    v_b = mix("v_b", [P, NB, WB])
    spare = mix.at
    late = Placed(nc, R + 8320)
    ob_hi = late("ob_hi", [P, 4, T], F32R)
    ob_lo = late("ob_lo", [P, 4, T], F32R)
    gate_a = late("gate_a", [P, KD, T])
    m_at = late.at
    ring = [late(f"ring{i}", [P, 512]) for i in range(3)] + [Placed(nc, spare)("ring3", [P, 512])]
    late = Placed(nc, work)
    beta = late("beta", [P, 2, 512])
    suffix = late("suffix", [P, 520])
    w_t = late("w_t", [P, 2, 512])
    keep = sqb[:, :, :].rearrange("p a b -> p (a b)")[:, 0:512]
    values = Placed(nc, work)
    va_1 = values("va_1", [P, DEC, 256])
    va_23 = values("va_23", [83, DEC, 256])
    blocks = ring + [Placed(nc, work + 2048 * i)(f"block{i}", [P, 512]) for i in range(8)]
    s_a = Placed(nc, R + 54784)("s_a", [P, 2, 211])
    flat = lambda t: t[:, :, :].rearrange("p a b -> p (a b)")
    s_beta = flat(sqa)[:, 0:512].rearrange("p (r k) -> p r k", r=2)
    s_keep = flat(sqa)[:, 512:1024].rearrange("p (r k) -> p r k", r=2)
    s_suffix = flat(tmp)[:, 0:514].rearrange("p (r k) -> p r k", r=2)
    pt_a = flat(acc)[:, 0:512].rearrange("p (n c) -> p n c", c=P)
    pt_b = flat(root)[:, 0:512].rearrange("p (n c) -> p n c", c=P)
    folded = [flat(tmp)[:, 0:512], flat(sqa)[:, 0:512], flat(sqa)[:, 512:1024]]
    end = Placed(nc, m_at)
    m_hi = end("m_hi", [P, KD, T], F32R)
    m_lo = end("m_lo", [P, KD, T], F32R)
    gate_b = end("gate_b", [P, KD, T])
    assert dist1 is not None and max(ffn.at, spare + 2048, end.at) <= nc.sbuf_usable_end

    sqh = [sqb[:, 0, :], sqb[:, 1, :], sqa[:, 0, :], sqa[:, 1, :]]
    m_tmp = [tmp[:, 0, :], tmp[:, 1, :], sqb[:, 0, :], sqb[:, 1, :]]

    psum = [nc.alloc_psum_tensor(f"bank{i}", [P, 512], F32) for i in range(8)]
    bank = psum[0:4]
    sum_post, sum_pre = psum[4:6], psum[6:8]
    s1, s2, tb, ob = psum[4:8]

    ctx = ExitStack()

    def sem(name):
        return ctx.enter_context(nc.semaphore(name))

    with ctx:
        cst_in = sem("cst_in")
        const_in = sem("const_in")
        x_in = [sem(f"x_in{i}") for i in range(8)]
        raw_in = [sem("raw_in0"), sem("raw_in1")]
        hi_made = sem("hi_made")
        lo_made = sem("lo_made")
        part_used = sem("part_used")
        full = [sem(f"full{b}") for b in range(4)]
        read = [sem(f"read{b}") for b in range(4)]
        consts_ready = sem("consts_ready")
        hid_made = sem("hid_made")
        post_sq = sem("post_sq")
        acc_added = sem("acc_added")
        post_summed = sem("post_summed")
        h_sq = sem("h_sq")
        h_summed = sem("h_summed")
        root_made = sem("root_made")
        post_rinv = sem("post_rinv")
        f_scaled = sem("f_scaled")
        pre_rinv = sem("pre_rinv")
        hn_pool = sem("hn_pool")
        hi_half = sem("hi_half")
        h_ready = sem("h_ready")
        hn_made = sem("hn_made")
        uh_made = sem("uh_made")
        u_made = sem("u_made")
        mix_in = sem("mix_in")
        mix_ready = sem("mix_ready")
        v_turned = sem("v_turned")
        v_placed = sem("v_placed")
        a_scored = sem("a_scored")
        a_biased = sem("a_biased")
        a_max = sem("a_max")
        a_exp = sem("a_exp")
        a_prob = sem("a_prob")
        a_turned = sem("a_turned")
        a_pt_act = sem("a_pt_act")
        a_pt_dve = sem("a_pt_dve")
        a_out = sem("a_out")
        a_hi = sem("a_hi")
        a_lo = sem("a_lo")
        b_scored = sem("b_scored")
        b_beta = sem("b_beta")
        b_weight = sem("b_weight")
        b_turned = sem("b_turned")
        b_wt = sem("b_wt")
        b_out = sem("b_out")
        b_hi = sem("b_hi")
        b_lo = sem("b_lo")
        ring_in = [sem(f"ring_in{i}") for i in range(4)]
        page_in = [sem(f"page_in{i}") for i in range(8)]
        page_used = sem("page_used")
        ring_used = sem("ring_used")
        va_in = sem("va_in")
        va_used = sem("va_used")
        fold_copied = sem("fold_copied")
        fold_turned = sem("fold_turned")
        self_in = sem("self_in")
        s_zero = sem("s_zero")
        s_scored = sem("s_scored")
        s_bias = sem("s_bias")
        s_max = sem("s_max")
        s_exp = sem("s_exp")
        s_sig = sem("s_sig")
        s_prob = sem("s_prob")
        s_turned = sem("s_turned")
        s_pt = sem("s_pt")
        sb_out = sem("sb_out")
        s_hi = sem("s_hi")
        s_lo = sem("s_lo")
        pool_own = sem("pool_own")
        qz_made = sem("qz_made")
        m_sum = sem("m_sum")
        m_top = sem("m_top")
        m_made = sem("m_made")
        vs_out = sem("vs_out")
        ka_out = sem("ka_out")
        kb_out = sem("kb_out")
        va_out = sem("va_out")
        vb_out = sem("vb_out")
        stored = sem("stored")
        block = ctx.enter_context(nc.Block())

        def tg(g):
            return slice(g * TG, (g + 1) * TG)

        def out_of(b):
            return bank[b][:, 0:TG]

        def fold_view(src, n):
            return src[:].rearrange("p (t r j c) -> p t r j c", t=n, r=4 // n, c=32)

        def sample_columns(dst, r=None):
            s0 = SEQ if r is None else SEQ + 4 * r
            s1_ = T if r is None else s0 + 4
            return dst[:, 0:2 if r is None else 4, s0:s1_].rearrange("p t (r j) -> p t r j", j=4)

        def wait_chunk_used(eng, n):
            if n < FFN1 + 2 * UPS:
                eng.wait_ge(full[3], R_FFN1 + n - FFN1 + 1)
            elif n < QKV:
                r, kc = divmod(n - 2 * UPS, KC)
                if kc < KC - 1:
                    eng.wait_ge(part_used, (KC - 1) * r + kc + 1)
                else:
                    eng.wait_ge(full[3], R_FFN1 + 2 * UPS + r + 1)
            elif n < PA:
                eng.wait_ge(full[3], R_QKV + n - QKV + 1)
            elif n == PA:
                eng.wait_ge(full[3], R_PA + 4)
            elif n < WO:
                eng.wait_ge(full[3], R_PB + 2 * (n - PB) + 2)
            elif n < FFN2:
                eng.wait_ge(full[3], R_WO + n - WO + 1)
            elif n < FFN2 + 2 * UPS:
                eng.wait_ge(full[3], R_FFN2 + n - FFN2 + 1)
            else:
                r, kc = divmod(n - FFN2 - 2 * UPS, KC)
                if kc < KC - 1:
                    eng.wait_ge(part_used, (KC - 1) * (DNS + r) + kc + 1)
                else:
                    eng.wait_ge(full[3], R_FFN2 + 2 * UPS + r + 1)

        def post_root(p, g):
            return 3 + 4 * p + 2 * g if p < 2 else 11 + g

        def pre_root(q, g):
            return g + 1 if q == 0 else 4 * q + 2 * g

        def hn_at(q, g):
            return 2 + 2 * (2 * q + g) if q or g else 0

        def out_at(p, r, b):
            if p == 1 and r >= DNS - 2:
                return 16 + 4 * (DNS - 2) + 4 * (b // 2) + 2 * (r - DNS + 2) + b % 2
            return 16 * p + 4 * r + b

        def m2_pieces(u):
            return [j // 2 for j in range(3 * u, 3 * u + 3) if j % 2]

        @block.sync
        def _(sp):
            def load(n, slot, size=CH):
                src = w_stream[n] if isinstance(n, int) else w_stream[bass.ds(n, 1)].rearrange("a p c -> (a p) c")
                sp.dma_start(raw[:, slot, 0:size], src[:, 0:size]).then_inc(raw_in[slot], 16)

            def load_next(n):
                if n >= CHUNKS:
                    return
                sp.wait_ge(lo_made, n - 1)
                start = FFN1 if n < QKV else FFN2
                down = n - start - 2 * UPS
                short = down >= 0 and (n < QKV or n >= FFN2) and down % KC == KC - 1
                load(n, n % 2, (KF - KD * (KC - 1)) * CW if short else CH)

            def ffn_loads(n0):
                with sp.Fori(0, UPS - 1) as i:
                    for s in range(2):
                        sp.wait_ge(lo_made, n0 + 2 * i + 1 + s)
                        load(n0 + 2 * i + 2 + s, s)
                for n in range(n0 + 2 * UPS, n0 + 2 * UPS + DNS * KC):
                    load_next(n)

            for g in range(G):
                for s in range(4):
                    part = (slice(None), slice(2 * s, 2 * s + 2), tg(g))
                    sp.dma_start(h[part], x_t[part]).then_inc(x_in[4 * g + s], 16)
                    if g == 0 and s == 0:
                        sp.dma_start(cst[:], consts[:, 0:2 * P]).then_inc(cst_in, 16)
                if g == 0:
                    load(0, 0)
                    sp.dma_start(gain[:], gains_in).then_inc(const_in, 16)
                    sp.dma_start(bias_b[:], b_rows).then_inc(const_in, 16)
                    sp.dma_start(pg[0:1, :], pages).then_inc(const_in, 16)
            load(1, 1)
            ffn_loads(FFN1)
            load_next(QKV)
            load_next(QKV + 1)
            sp.wait_ge(full[3], R_QKV)
            at = 2 * P
            for table, width in ((dist1, 515), (dist2, P), (dist3, P), (tri, P)):
                sp.dma_start(table[:, 0:width], consts[:, at:at + width]).then_inc(mix_in, 16)
                at += width

            def store_k(c):
                sp.wait_ge(read[3], R_QKV + c + 1)
                if c == 3:
                    sp.dma_start(ka1_t, k_a[:, 0:2, SEQ - P:T]).then_inc(ka_out, 16)
                elif c < 6:
                    out = ka2_t if c == 4 else ka3_t
                    sp.dma_start(out, k_a[:, 2 * (c - 3):2 * (c - 3) + 2, :]).then_inc(ka_out, 16)
                else:
                    j = 2 * (c - 11)
                    sp.dma_start(kb_t[:, j:j + 2, :], k_b[:, j:j + 2, :]).then_inc(kb_out, 16)

            def store_v_sample(n, c):
                sp.wait_ge(read[3], R_QKV + c + 1)
                sp.dma_start(vs_t[:, 2 * n:2 * n + 2, :], vt[:, :, SEQ:T]).then_inc(vs_out, 16)

            def store_v(n):
                sp.wait_ge(v_placed, 3 * (n + 1) if n < 3 else 9 + 2 * (n - 2))
                if n == 0:
                    sp.dma_start(va1_o, v_a[:, NB - 1, 0:256]).then_inc(va_out, 16)
                elif n < 3:
                    out = va2_o if n == 1 else va3_o
                    sp.dma_start(out, v_a[:, :, n * 256:(n + 1) * 256]).then_inc(va_out, 16)
                else:
                    j = (n - 3) * 256
                    sp.dma_start(vb_o[:, :, j:j + 256], v_b[:, :, j:j + 256]).then_inc(vb_out, 16)

            for n in range(QKV + 2, GB):
                load_next(n)
                c = n - QKV - 3
                if c in (3, 4, 5, 11, 12):
                    store_k(c)
                if c in (6, 7, 8, 13, 14):
                    v = c - 6 if c < 9 else c - 10
                    store_v_sample(v, c)
                if c in (7, 8, 9, 14, 15):
                    store_v(c - 7 if c < 10 else c - 11)
            sp.wait_ge(const_in, 48)
            def page(pool_t, x, slot, sem_in):
                r = sp.value_load(pg[0:1, x:x + 1], min_val=0, max_val=kb_pool.shape[0] - 1)
                sp.dma_start(slot[:], pool_t[bass.ds(r, 1)].rearrange("a p c -> (a p) c")).then_inc(sem_in, 16)

            def load_keys_a(x):
                if x >= 4:
                    sp.wait_ge(ring_used, x - 3)
                sp.dma_start(ring[x % 4][:, 0:422], ka_cache[x]).then_inc(ring_in[x % 4], 16)

            def load_key_pages(y0, y1):
                for y in range(y0, y1):
                    if y >= 8:
                        sp.wait_ge(ring_used, y - 3)
                    page(kb_pool, y, ring[y % 4] if y >= 8 else blocks[4 + y], (ring_in[y % 4] if y >= 8 else page_in[y]))

            def load_value_pages(y0, y1):
                for y in range(y0, y1):
                    if y < 4:
                        sp.wait_ge(ring_used, 13 + y)
                    elif y == 4:
                        sp.wait_ge(va_used, 1)
                    elif y >= 12:
                        sp.wait_ge(ring_used, 17 + y - 12)
                    page(vb_pool, y, blocks[y % 12], page_in[y - 4] if 4 <= y < 12 else ring_in[y % 4])

            load_next(GB)
            load_next(GB + 1)
            sp.wait_ge(v_turned, 13)
            sp.wait_ge(vs_out, 80)
            sp.wait_ge(va_out, 48)
            sp.wait_ge(a_biased, AH * 4 * 3)
            sp.dma_start(s_a[:, :, :].rearrange("p r k -> p (r k)"), sample_bias).then_inc(s_bias, 16)
            for x in range(4):
                load_keys_a(x)
            load_next(GB + 2)
            sp.wait_ge(b_out, 32)
            load_key_pages(0, 2)
            for x in range(4, 8):
                load_keys_a(x)
            load_key_pages(2, 8)
            load_next(GB + 3)
            load_key_pages(8, 12)
            sp.wait_ge(page_used, 8)
            sp.dma_start(va_1[:], va_cache1).then_inc(va_in, 16)
            load_key_pages(12, 14)
            sp.dma_start(va_23[1:65], va_cache2[0:64]).then_inc(va_in, 16)
            sp.dma_start(va_23[66:82], va_cache2[64:80]).then_inc(va_in, 16)
            for g, row in enumerate((0, 65, 82)):
                sp.dma_start(va_23[row:row + 1], v_self[:, g * 256:(g + 1) * 256]).then_inc(va_in, 16)
            load_key_pages(14, 16)
            load_next(GB + 4)
            load_value_pages(0, 12)
            load_next(GB + 5)
            load_value_pages(12, 16)
            for n in range(GB + 6, FFN2 + 2):
                load_next(n)
            ffn_loads(FFN2)
            for g in range(G):
                for s in range(4):
                    part = (slice(None), slice(2 * s, 2 * s + 2), tg(g))
                    sp.wait_ge(h_ready, 16 + 4 * g + s + 1)
                    sp.dma_start(y_t[part], h[part]).then_inc(stored, 16)
            sp.wait_ge(stored, 8 * 16)
            sp.wait_ge(ka_out, 48)
            sp.wait_ge(kb_out, 32)
            sp.wait_ge(va_out, 48)
            sp.wait_ge(vb_out, 32)
            sp.wait_ge(vs_out, 80)

        @block.gpsimd
        def _(pool):
            def lo(n, slot):
                pool.wait_ge(hi_made, n + 1)
                pool.tensor_tensor(w_lo[:, slot, :], raw[:, slot, :], w_hi[:, slot, :].bitcast(F32),
                                   ALU.subtract).then_inc(lo_made, 1)

            def los(n0, n1):
                for n in range(n0, n1):
                    lo(n, n % 2)

            def scale_f(p, g):
                pool.wait_ge(post_rinv, 2 * p + g + 1)
                for s in range(2, 4):
                    part = f[:, 2 * s:2 * s + 2, tg(g)]
                    pool.tensor_tensor(part, part, rinv[:, g:g + 1, :].to_broadcast([P, 2, TG]),
                                       ALU.mult).then_inc(f_scaled, 1)

            def scale_h(q, g):
                pool.wait_ge(pre_rinv, 2 * q + g)
                for s in range(2, 4):
                    part = (slice(None), slice(2 * s, 2 * s + 2), tg(g))
                    pool.tensor_tensor(f[part], h[part], rinv[:, g:g + 1, :].to_broadcast([P, 2, TG]),
                                       ALU.mult).then_inc(hn_pool, 1)

            def boundary(p, n):
                scale_f(p, 0)
                if n < CHUNKS:
                    lo(n, 0)
                    scale_h(p + 1, 0)
                    lo(n + 1, 1)
                scale_f(p, 1)
                if n < CHUNKS:
                    scale_h(p + 1, 1)
                    lo_by_halves(n + 2, (3, 4)[p])
                    lo(n + 3, 1)

            def lo_by_halves(n, count):
                pool.wait_ge(hi_half, count)
                a, half = n % 2, CH // 2
                pool.tensor_tensor(w_lo[:, a, 0:half], raw[:, a, 0:half], w_hi[:, a, 0:half].bitcast(F32),
                                   ALU.subtract)
                pool.wait_ge(hi_made, n + 1)
                pool.tensor_tensor(w_lo[:, a, half:CH], raw[:, a, half:CH], w_hi[:, a, half:CH].bitcast(F32),
                                   ALU.subtract).then_inc(lo_made, 1)

            lo(0, 0)
            lo(1, 1)
            scale_h(0, 1)
            lo_by_halves(2, 1)
            lo(3, 1)
            with pool.Fori(2, QKV // 2 - 1) as i:
                lo(2 * i, 0)
                lo(2 * i + 1, 1)
            lo(QKV - 2, 0)
            lo_by_halves(QKV - 1, 2)
            boundary(0, QKV)
            pool.wait_ge(full[3], R_QKV)
            pool.memset(qz_a[:], 0.0).then_inc(pool_own, 1)
            pool.memset(qz_b[:], 0.0).then_inc(pool_own, 1)
            los(QKV + 4, QKV + 5)
            los(QKV + 5, QKV + 8)
            pool.wait_ge(read[3], R_QKV + 6)
            pool.tensor_copy(k_self[:], k_a[:, :, SEQ:T]).then_inc(pool_own, 1)
            los(QKV + 8, QKV + 13)
            los(QKV + 13, GB + 1)
            pool.wait_ge(pool_own, 3)
            for b in range(DEC):
                if b == 4:
                    lo(GB + 1, 0)
                pool.wait_ge(ring_in[b % 4], 16 * (b // 4 + 1))
                for g, col in enumerate((128, 193, 210)):
                    dst = ring[b % 4][:, 0:422].rearrange("p (t k) -> p t k", t=2)
                    pool.tensor_copy(dst[:, :, col], k_self[:, 2 * g:2 * g + 2, b]).then_inc(self_in, 1)
            los(GB + 2, FFN2)
            boundary(1, FFN2)
            with pool.Fori(0, (CHUNKS - FFN2 - 6) // 2) as i:
                lo(2 * i + FFN2 + 4, 0)
                lo(2 * i + FFN2 + 5, 1)
            lo(CHUNKS - 2, 0)
            lo_by_halves(CHUNKS - 1, 5)
            boundary(2, CHUNKS)

        @block.scalar
        def _(act):
            def hi_copy(slot):
                act.activation(w_hi[:, slot, :], raw[:, slot, :], ACT.Copy).then_inc(hi_made, 1)

            def hi(n):
                if n >= CHUNKS:
                    return
                act.wait_ge(raw_in[n % 2], 16 * (n // 2 + 1))
                if n >= 2:
                    wait_chunk_used(act, n - 2)
                hi_copy(n % 2)

            def hi_by_halves(n):
                act.wait_ge(raw_in[n % 2], 16 * (n // 2 + 1))
                wait_chunk_used(act, n - 2)
                half = CH // 2
                act.activation(w_hi[:, n % 2, 0:half], raw[:, n % 2, 0:half], ACT.Copy).then_inc(hi_half, 1)
                act.activation(w_hi[:, n % 2, half:CH], raw[:, n % 2, half:CH], ACT.Copy).then_inc(hi_made, 1)

            def square_h(q, g):
                for t in range(KD):
                    c = 16 * q + 8 * g + t
                    if q == 0:
                        act.wait_ge(x_in[4 * g + t // 2], 16)
                    else:
                        act.wait_ge(h_ready, 8 * (q - 1) + 4 * g + t // 2 + 1)
                    if c >= 4:
                        act.wait_ge(h_summed, c - 3)
                    act.activation(sqh[t % 4], h[:, t, tg(g)], ACT.Square).then_inc(h_sq, 1)

            def warm_sqrt():
                act.activation(warm[:], eps[:], ACT.Sqrt)

            def take_root(src, summed, count, g):
                act.wait_ge(summed, count)
                act.activation(root[:, g, :], src[g][:, 0:TG], ACT.Sqrt, bias=eps[:, 0:1],
                               scale=1.0 / D).then_inc(root_made, 1)

            def u_top(q, g):
                for t in range(KD):
                    if t % 2 == 0:
                        if t < 4 or (q, g) == (0, 0):
                            act.wait_ge(hn_made, hn_at(q, g) + t // 2 + 1)
                        else:
                            act.wait_ge(hn_pool, 2 * (2 * q + g - 1) + t // 2 - 1)
                    act.activation(u_hi[:, t, tg(g)], f[:, t, tg(g)], ACT.Copy,
                                   scale=gain[:, 2 * q, t:t + 1]).then_inc(uh_made, 1)

            def square_out(p, r0, r, b):
                act.wait_ge(full[b], r0 + r + 1)
                if r:
                    act.wait_ge(acc_added, out_at(p, r - 1, b) + 1)
                elif p:
                    act.wait_ge(acc_added, out_at(p - 1, DNS - 1, b) + 1)
                act.activation(sqa[:, b, :], out_of(b), ACT.Square).then_inc(post_sq, 1)

            def next_group(q, read_out):
                read_out(0)
                read_out(1)
                warm_sqrt()
                square_h(q, 1)
                take_root(sum_pre, h_summed, 16 * q + 16, 1)
                u_top(q, 1)
                read_out(2)
                read_out(3)

            def boundary(p, r0, n, read_out):
                for r in range(DNS - 2 if p == 1 else DNS - 1, DNS):
                    for b in range(2):
                        square_out(p, r0, r, b)
                take_root(sum_post, post_summed, 2 * p + 1, 0)
                if p == 1:
                    square_out(p, r0, DNS - 2, 2)
                    square_out(p, r0, DNS - 2, 3)
                hi(n)
                if p < 2:
                    square_h(p + 1, 0)
                square_out(p, r0, DNS - 1, 2)
                if p < 2:
                    take_root(sum_pre, h_summed, 16 * (p + 1) + 8, 0)
                square_out(p, r0, DNS - 1, 3)
                hi(n + 1)
                if p < 2:
                    u_top(p + 1, 0)
                take_root(sum_post, post_summed, 2 * p + 2, 1)
                if p < 2:
                    next_group(p + 1, read_out)

            def silu_out(b, r):
                act.wait_ge(full[b], r)
                act.activation(sg[:, b, :], out_of(b), ACT.Silu).then_inc(read[b], 1)

            def ffn_up(n0, r0):
                hi_by_halves(n0 + 2)
                hi(n0 + 3)
                with act.Fori(1, UPS) as i:
                    for b in range(4):
                        silu_out(b, r0 + 1 + 2 * i)
                    for s in range(2):
                        act.wait_ge(raw_in[s], n0 * 8 + 32 + 16 * i)
                        act.wait_ge(full[3], r0 + 1 + s + 2 * i)
                        hi_copy(s)

            def outputs(p, r0, n0, kc, read_out):
                for r in range(DNS - 2 if p == 1 else DNS - 1):
                    n = n0 + kc * r
                    for j in range(kc - 1):
                        hi(n + j + 2)
                    for b in range(4):
                        square_out(p, r0, r, b)
                    hi(n + kc + 1)
                    if r == 0:
                        warm_sqrt()
                if p != 1:
                    hi_by_halves(n0 + kc * DNS - 1)
                boundary(p, r0, n0 + kc * DNS, read_out)

            def project_out(c, b):
                g, t = divmod(b, 2)
                act.wait_ge(full[b], R_QKV + c + 1)
                kind, j = (c // 3, c % 3) if c < 9 else ((c - 9) // 2, (c - 9) % 2)
                if kind == 2:
                    v = c - 6 if c < 9 else c - 10
                    if b == 0 and v:
                        act.wait_ge(v_turned, 3 * v if v < 4 else 11)
                        act.wait_ge(vs_out, 16 * v)
                    dst, scale = vt[:, t, tg(g)], 1.0
                else:
                    dst = ((q_a, k_a) if c < 9 else (q_b, k_b))[kind][:, 2 * j + t, tg(g)]
                    scale = SCALE if kind == 0 else 1.0
                act.activation(dst, out_of(b), ACT.Copy, scale=scale).then_inc(read[b], 1)

            act.wait_ge(consts_ready, 1)
            warm_sqrt()
            square_h(0, 0)
            hi(0)
            take_root(sum_pre, h_summed, 8, 0)
            square_h(0, 1)
            act.wait_ge(consts_ready, 3)
            u_top(0, 0)
            take_root(sum_pre, h_summed, 16, 1)
            hi(1)
            u_top(0, 1)
            for b in range(4):
                silu_out(b, R_FFN1 + 1)
            ffn_up(FFN1, R_FFN1)
            outputs(0, R_FFN1 + 2 * UPS, FFN1 + 2 * UPS, KC, lambda b: project_out(0, b))

            def spread_q(dst, src, tiles, r):
                act.wait_ge(read[3], r)
                for half in range(2):
                    rows = slice(64 * half, 64 * half + 64)
                    for i in range(tiles):
                        hd = 2 * (i % 2 if tiles == 6 else i) + half
                        act.activation(dst[rows, i, :, hd], src[rows, i, SEQ:T], ACT.Copy).then_inc(qz_made, 1)

            for c in range(9):
                for b in range(4 if c else 0):
                    project_out(c, b)
                if c == 3:
                    act.wait_ge(pool_own, 2)
                    spread_q(qz_a, q_a, 6, R_QKV + 3)
                (hi if c else hi_by_halves)(QKV + c + 2)

            def a_where(u):
                r, hd = divmod(u, AH)
                return r, hd // 2, 64 * (hd % 2)

            def a_expo(u):
                act.wait_ge(a_max, u + 1)
                act.activation(sc[:, u % 2, :], sc[:, u % 2, :], ACT.Exp, bias=stat[:, 2 + u % 2:3 + u % 2],
                               accum_out=stat[:, 4 + u % 2:5 + u % 2]).then_inc(a_exp, 1)

            def a_top(u):
                r, t, po = a_where(u)
                act.wait_ge(a_out, u + 1)
                act.activation(oa_hi[po:po + 64, t, r:SEQ:4], ob[po:po + 64, 0:P], ACT.Copy).then_inc(a_hi, 1)

            a_expo(0)
            for u in range(16):
                if u >= 2:
                    a_top(u - 2)
                if u + 1 < 16:
                    a_expo(u + 1)
                for j in m2_pieces(u):
                    project_out(9 + j // 4, j % 4)
                act.wait_ge(a_turned, u + 1)
                if u >= 2:
                    act.wait_ge(a_out, u - 1)
                act.activation(p_t[:, u % 2, 0:512], tb[:], ACT.Copy).then_inc(a_pt_act, 1)
                for j in m2_pieces(u):
                    if j % 4 == 3:
                        hi(QKV + 9 + j // 4 + 2)
                if u == 8:
                    spread_q(qz_b, q_b, 4, R_QKV + 11)
            a_top(14)
            a_top(15)

            def b_sigmoid(w):
                hd, i = divmod(w, NB)
                act.wait_ge(b_scored, w + 1)
                if w >= 2:
                    act.wait_ge(b_turned, w - 1)
                n = (i + 1) * P
                act.activation(beta[:, w % 2, 0:n], (s1, s2)[w % 2][:, 0:n], ACT.Sigmoid,
                               bias=bias_b[:, hd:hd + 1]).then_inc(b_beta, 1)

            def b_top(w):
                hd, i = divmod(w, NB)
                po = 64 * (hd % 2)
                act.wait_ge(b_out, w + 1)
                act.activation(ob_hi[po:po + 64, hd // 2, i * P:(i + 1) * P], ob[po:po + 64, 0:P],
                               ACT.Copy).then_inc(b_hi, 1)

            def gate_out(dst, r0, j):
                c, b = divmod(j, 4)
                act.wait_ge(full[b], r0 + c + 1)
                act.activation(dst[:, 2 * c + b % 2, tg(b // 2)], out_of(b), ACT.Sigmoid).then_inc(read[b], 1)

            def hi_part(n, x):
                if x == 0:
                    act.wait_ge(raw_in[n % 2], 16 * (n // 2 + 1))
                    wait_chunk_used(act, n - 2)
                part = slice(x * CH // 2, (x + 1) * CH // 2)
                split = act.activation(w_hi[:, n % 2, part], raw[:, n % 2, part], ACT.Copy)
                if x == 1:
                    split.then_inc(hi_made, 1)

            b_sigmoid(0)
            act.wait_ge(ka_out, 48)
            act.wait_ge(va_out, 48)
            for w in range(32):
                if w >= 2:
                    b_top(w - 2)
                if w + 1 < 32:
                    b_sigmoid(w + 1)
                if w % 2 == 1:
                    gate_out(gate_a, R_GA, w // 2)
                act.wait_ge(b_turned, w + 1)
                if w >= 2:
                    act.wait_ge(b_out, w - 1)
                n = (w % NB + 1) * P
                act.activation(w_t[:, w % 2, 0:n], tb[:, 0:n], ACT.Copy).then_inc(b_wt, 1)
                if w % 8 in (4, 6):
                    hi_part(GA + w // 8 + 2, w % 8 // 2 - 2)
            b_top(30)
            b_top(31)
            act.wait_ge(kb_out, 32)
            act.wait_ge(vb_out, 32)
            def fold_copy(x, src):
                act.activation(folded[x], src[:], ACT.Copy).then_inc(fold_copied, 1)

            def fold_top(x, src, dst, n):
                act.wait_ge(fold_turned, x + 1)
                for half in range(2):
                    rows = slice(64 * half, 64 * half + 64)
                    act.activation(dst[rows], fold_view(src, n)[rows, :, :, :, half], ACT.Copy).then_inc(s_hi, 1)

            for j in range(16):
                gate_out(gate_b, R_GB, j)
                if j == 4:
                    act.wait_ge(s_max, 1)
                    for r in range(2):
                        act.activation(s_a[:, r, :], s_a[:, r, :], ACT.Exp, bias=stat[:, 10 + r:11 + r],
                                       accum_out=stat[:, 12 + r:13 + r]).then_inc(s_exp, 1)
                if j == 7:
                    act.wait_ge(s_turned, 1)
                    turned = tb[:].rearrange("p (r n c) -> p r n c", r=2, n=2)
                    dst = pt_a.rearrange("p (r n) c -> p r n c", r=2)
                    act.activation(dst[:, :, 0, :], turned[:, :, 0, :], ACT.Copy).then_inc(s_pt, 1)
                    act.activation(dst[0:83, :, 1, :], turned[0:83, :, 1, :], ACT.Copy).then_inc(s_pt, 1)
                if j == 8:
                    act.wait_ge(ring_used, 16)
                    act.activation(s_beta.rearrange("p r k -> p (r k)"), s2[:], ACT.Sigmoid,
                                   bias=bias_b[:, BH:BH + 1]).then_inc(s_sig, 1)
                if j == 11:
                    act.wait_ge(s_turned, 2)
                    act.activation(pt_b.rearrange("p n c -> p (n c)"), ob[:], ACT.Copy).then_inc(s_pt, 1)
                    act.wait_ge(s_prob, 3)
                    fold_copy(0, s1)
                if j == 13:
                    fold_top(0, tb, sample_columns(oa_hi), 2)
                if j == 14:
                    act.wait_ge(sb_out, 1)
                    fold_copy(1, s2)
                if j % 4 == 3:
                    hi(GB + j // 4 + 2)
            act.wait_ge(sb_out, 2)
            fold_copy(2, ob)
            for x in range(2):
                fold_top(1 + x, (s1, s2)[x], sample_columns(ob_hi, x), 4)
            hi(PA + 2)

            def m_round(x):
                act.wait_ge(m_sum, x + 1)
                r, b = divmod(x, 4)
                act.activation(m_hi[:, 2 * r + b % 2, tg(b // 2)], m_tmp[x % 4], ACT.Copy).then_inc(m_top, 1)

            for x in range(16):
                m_round(x)
                if x % 8 == 7:
                    hi(PB + x // 8 + 2)
            outputs(1, R_WO, WO, 1, lambda b: silu_out(b, R_FFN2 + 1))
            ffn_up(FFN2, R_FFN2)
            outputs(2, R_FFN2 + 2 * UPS, FFN2 + 2 * UPS, KC, None)

        @block.vector
        def _(dve):
            def drain():
                dve.drain()

            def u_scale(q, g):
                dve.wait_ge(root_made, pre_root(q, g))
                drain()
                recip = dve.reciprocal(rinv[:, g, :], root[:, g, :])
                if q or g:
                    recip.then_inc(pre_rinv, 1)
                drain()
                for s in range(2 if q or g else 4):
                    part = (slice(None), slice(2 * s, 2 * s + 2), tg(g))
                    dve.tensor_tensor(f[part], h[part], rinv[:, g:g + 1, :].to_broadcast([P, 2, TG]),
                                      ALU.mult).then_inc(hn_made, 1)
                drain()

            def u_low(q, g, tiles=range(KD)):
                for t in tiles:
                    dve.wait_ge(uh_made, 16 * q + 8 * g + t + 1)
                    dve.scalar_tensor_tensor(u_lo[:, t, tg(g)], f[:, t, tg(g)], gain[:, 2 * q, t:t + 1],
                                             u_hi[:, t, tg(g)].bitcast(F32), ALU.mult,
                                             ALU.subtract).then_inc(u_made, 1)

            def h_of(p, g, between=None):
                dve.wait_ge(root_made, post_root(p, g))
                drain()
                dve.reciprocal(rinv[:, g, :], root[:, g, :]).then_inc(post_rinv, 1)
                drain()
                for s in range(2):
                    part = f[:, 2 * s:2 * s + 2, tg(g)]
                    dve.tensor_tensor(part, part, rinv[:, g:g + 1, :].to_broadcast([P, 2, TG]), ALU.mult)
                if between is not None:
                    between()
                drain()
                for s in range(4):
                    if s >= 2:
                        dve.wait_ge(f_scaled, 2 * (2 * p + g) + s - 1)
                    part = h[:, 2 * s:2 * s + 2, tg(g)]
                    dve.tensor_tensor(part, part, f[:, 2 * s:2 * s + 2, tg(g)], ALU.add).then_inc(h_ready, 1)

            def take_out(p, r, b):
                g, t = divmod(b, 2)
                dve.wait_ge(post_sq, out_at(p, r, b) + 1)
                dve.tensor_scalar(f[:, 2 * r + t, tg(g)], out_of(b), gain[:, 2 * p + 1, 2 * r + t:2 * r + t + 1],
                                  None, ALU.mult).then_inc(read[b], 1)
                if r == 0 and t == 0:
                    dve.tensor_copy(acc[:, g, :], sqa[:, b, :]).then_inc(acc_added, 1)
                else:
                    dve.tensor_tensor(acc[:, g, :], acc[:, g, :], sqa[:, b, :], ALU.add).then_inc(acc_added, 1)
                drain()

            def outputs(p):
                last = DNS - 2 if p == 1 else DNS - 1
                for r in range(last):
                    for b in range(4):
                        take_out(p, r, b)
                for r in range(last, DNS):
                    take_out(p, r, 0)
                    take_out(p, r, 1)
                h_of(p, 0, (lambda: take_out(p, DNS - 2, 2)) if p == 1 else None)
                if p == 1:
                    take_out(p, DNS - 2, 3)
                take_out(p, DNS - 1, 2)
                if p < 2:
                    u_scale(p + 1, 0)
                if p < 2:
                    u_low(p + 1, 0, range(KD // 2))
                take_out(p, DNS - 1, 3)
                if p < 2:
                    u_low(p + 1, 0, range(KD // 2, KD))
                h_of(p, 1)
                if p < 2:
                    u_scale(p + 1, 1)
                    u_low(p + 1, 1)

            def ffn_up(r0):
                with dve.Fori(0, UPS) as i:
                    for b in range(4):
                        g, t = divmod(b, 2)
                        dve.wait_ge(full[b], r0 + 2 + 2 * i)
                        x = tmp[:, b % 2, :]
                        dve.tensor_tensor(x, sg[:, b, :], out_of(b), ALU.mult).then_inc(read[b], 1)
                        drain()
                        top = hid_hi[:, bass.ds(2 * i + t, 1), tg(g)].rearrange("p a c -> p (a c)")
                        dve.tensor_copy(top, x)
                        drain()
                        low = hid_lo[:, bass.ds(2 * i + t, 1), tg(g)].rearrange("p a c -> p (a c)")
                        dve.tensor_tensor(low, x, top.bitcast(F32), ALU.subtract).then_inc(hid_made, 1)

            dve.memset(eps[:], EPS).then_inc(consts_ready, 1)
            dve.wait_ge(const_in, 48)
            for site in (1, 5):
                dve.tensor_scalar(gain[:, site, :], gain[:, site, :], 0.5, None, ALU.mult).then_inc(consts_ready, 1)
            for g in range(G):
                u_scale(0, g)
                u_low(0, g)
            ffn_up(R_FFN1)
            outputs(0)

            def place_v(n):
                dst = v_a[:, :, n * 256:(n + 1) * 256] if n < 3 else v_b[:, :, (n - 3) * 256:(n - 2) * 256]
                c = 3 * n if n < 4 else 11
                for t in range(2):
                    dve.wait_ge(v_turned, c + t + 1)
                    dve.tensor_copy(dst[:, :, t * P:(t + 1) * P],
                                    (tb, ob)[t][:].rearrange("p (k c) -> p k c", k=NB)).then_inc(v_placed, 1)

            def place_v_samples(n):
                dve.wait_ge(v_turned, 3 * n + 3)
                dve.tensor_copy(v_self[:, n * 256:(n + 1) * 256], tb[0:DEC, 0:256]).then_inc(v_placed, 1)

            for n in range(2):
                place_v(n)
                place_v_samples(n)
            dve.wait_ge(mix_in, 64)

            def a_bias(u):
                r, hd = divmod(u, AH)
                x = sc[:, u % 2, :]
                dve.wait_ge(a_scored, u + 1)
                if u >= 2:
                    dve.wait_ge(a_turned, u - 1)
                for g, (dst, src, dist) in enumerate(((x[:, 0:512], s1[:], dist1[:, 3 - r:515 - r]),
                                                      (x[:, 512:640], s2[:, 0:P], dist2[:]),
                                                      (x[:, 640:768], s2[:, P:2 * P], dist3[:]))):
                    dve.scalar_tensor_tensor(dst, dist, -slope(g, hd), src, ALU.mult, ALU.add).then_inc(a_biased, 1)
                drain()
                dve.tensor_reduce(stat[:, u % 2:u % 2 + 1], x, AX.X, ALU.max)
                drain()
                dve.tensor_scalar(stat[:, 2 + u % 2:3 + u % 2], stat[:, u % 2:u % 2 + 1], -1.0, None,
                                  ALU.mult).then_inc(a_max, 1)

            def a_norm(u):
                dve.wait_ge(a_exp, u + 1)
                dve.reciprocal(stat[:, 6 + u % 2:7 + u % 2], stat[:, 4 + u % 2:5 + u % 2])
                drain()
                dve.tensor_scalar(sc[:, u % 2, :], sc[:, u % 2, :], stat[:, 6 + u % 2:7 + u % 2], None,
                                  ALU.mult).then_inc(a_prob, 1)

            def a_low(u):
                r, hd = divmod(u, AH)
                t, po = hd // 2, 64 * (hd % 2)
                dve.wait_ge(a_hi, u + 1)
                dve.tensor_tensor(oa_lo[po:po + 64, t, r:SEQ:4], ob[po:po + 64, 0:P],
                                  oa_hi[po:po + 64, t, r:SEQ:4].bitcast(F32), ALU.subtract).then_inc(a_lo, 1)

            a_bias(0)
            for u in range(16):
                if u == 0:
                    place_v(2)
                a_norm(u)
                if u == 0:
                    place_v_samples(2)
                if u >= 2:
                    a_low(u - 2)
                if u + 1 < 16:
                    a_bias(u + 1)
                if u == 13:
                    place_v(3)
                dve.wait_ge(a_turned, u + 1)
                if u >= 2:
                    dve.wait_ge(a_out, u - 1)
                dve.tensor_copy(p_t[:, u % 2, 512:768], s2[:, 256:512]).then_inc(a_pt_dve, 1)
            a_low(14)
            a_low(15)

            def b_chain(w):
                i = w % NB
                n = (i + 1) * P
                x = beta[:, w % 2, 0:n]
                dve.wait_ge(b_beta, w + 1)
                dve.tensor_tensor(x[:, n - P:n], x[:, n - P:n], tri[:], ALU.mult)
                drain()
                dve.tensor_scalar(keep[:, 0:n], x, -1.0, 1.0, ALU.mult, ALU.add)
                drain()
                dve.tensor_tensor_scan(suffix[:, 512 - n:512][:, ::-1], keep[:, 0:n][:, ::-1], keep[:, 0:n], 1.0,
                                       ALU.mult, ALU.bypass)
                drain()
                dve.tensor_tensor(x, x, suffix[:, 513 - n:513], ALU.mult).then_inc(b_weight, 1)

            def b_low(w):
                hd, i = divmod(w, NB)
                po = 64 * (hd % 2)
                dve.wait_ge(b_hi, w + 1)
                dst = slice(i * P, (i + 1) * P)
                dve.tensor_tensor(ob_lo[po:po + 64, hd // 2, dst], ob[po:po + 64, 0:P],
                                  ob_hi[po:po + 64, hd // 2, dst].bitcast(F32), ALU.subtract).then_inc(b_lo, 1)

            dve.wait_ge(b_scored, 1)
            dve.memset(suffix[:, 512:513], 1.0)
            b_chain(0)
            for w in range(32):
                if w >= 2:
                    b_low(w - 2)
                if w == 1:
                    place_v(4)
                if w + 1 < 32:
                    b_chain(w + 1)
            dve.wait_ge(b_beta, 32)
            for score in (s1, s2):
                dve.memset(score[:], 0.0).then_inc(s_zero, 1)
            b_low(30)
            b_low(31)

            dve.memset(s_suffix[:, :, 256:257], 1.0)
            dve.wait_ge(s_bias, 16)
            dve.wait_ge(ring_used, 8)
            dve.tensor_tensor(s_a[:], s_a[:], s1[:, 0:422].rearrange("p (r k) -> p r k", r=2), ALU.add)
            drain()
            dve.tensor_reduce(stat[:, 8:10], s_a[:], AX.X, ALU.max)
            drain()
            dve.tensor_scalar(stat[:, 10:12], stat[:, 8:10], -1.0, None, ALU.mult).then_inc(s_max, 1)
            dve.wait_ge(s_exp, 2)
            dve.reciprocal(stat[:, 14:16], stat[:, 12:14])
            drain()
            for r in range(2):
                dve.tensor_scalar(s_a[:, r, :], s_a[:, r, :], stat[:, 14 + r:15 + r], None,
                                  ALU.mult).then_inc(s_prob, 1)
            dve.wait_ge(s_sig, 1)
            dve.tensor_scalar(s_keep, s_beta, -1.0, 1.0, ALU.mult, ALU.add)
            drain()
            for r in range(2):
                dve.tensor_tensor_scan(s_suffix[:, r, 0:256][:, ::-1], s_keep[:, r, :][:, ::-1], s_keep[:, r, :],
                                       1.0, ALU.mult, ALU.bypass)
            drain()
            dve.tensor_tensor(s_beta, s_beta, s_suffix[:, :, 1:257], ALU.mult).then_inc(s_prob, 1)

            def fold_low(k, src, hi_t, lo_t, n, r=None):
                for half in range(2):
                    rows = slice(64 * half, 64 * half + 64)
                    dve.wait_ge(s_hi, k + half + 1)
                    dve.tensor_tensor(sample_columns(lo_t, r)[rows], fold_view(src, n)[rows, :, :, :, half],
                                      sample_columns(hi_t, r)[rows].bitcast(F32), ALU.subtract).then_inc(s_lo, 1)

            fold_low(0, tb, oa_hi, oa_lo, 2)
            for r in range(2):
                fold_low(2 + 2 * r, (s1, s2)[r], ob_hi, ob_lo, 4, r)

            for x in range(16):
                r, b = divmod(x, 4)
                g, t = divmod(b, 2)
                part = gate_a[:, 2 * r + t, tg(g)]
                dve.wait_ge(full[b], R_PA + r + 1)
                dve.tensor_tensor(part, part, out_of(b), ALU.mult).then_inc(read[b], 1)
            drain()

            def m_low(x):
                r, b = divmod(x, 4)
                where = (slice(None), 2 * r + b % 2, tg(b // 2))
                dve.wait_ge(m_top, x + 1)
                dve.tensor_tensor(m_lo[where], m_tmp[x % 4], m_hi[where].bitcast(F32),
                                  ALU.subtract).then_inc(m_made, 1)

            for x in range(16):
                r, b = divmod(x, 4)
                where = (slice(None), 2 * r + b % 2, tg(b // 2))
                dve.wait_ge(full[b], R_PB + r + 1)
                dve.tensor_tensor(m_tmp[x % 4], gate_b[where], out_of(b), ALU.mult).then_inc(read[b], 1)
                drain()
                dve.tensor_tensor(m_tmp[x % 4], m_tmp[x % 4], gate_a[where], ALU.add).then_inc(m_sum, 1)
                if x:
                    m_low(x - 1)
            m_low(15)
            outputs(1)
            ffn_up(R_FFN2)
            outputs(2)

        @block.tensor
        def _(pe):
            def product(b, slot, kw, k, cols, x_hi, x_lo, kx, first, last):
                g = b // 2
                w = w_hi[:, slot, :].rearrange("p (k c) -> p k c", k=kw)[:, k, cols]
                v = w_lo[:, slot, :].rearrange("p (k c) -> p k c", k=kw)[:, k, cols]
                hi_x, lo_x = x_hi[:, kx, tg(g)], x_lo[:, kx, tg(g)]
                pe.matmul(out_of(b), w, hi_x, start=first, stop=False)
                pe.matmul(out_of(b), w, lo_x, start=False, stop=False)
                return pe.matmul(out_of(b), v, hi_x, start=False, stop=last)

            def tile_cols(b):
                t = b % 2
                return slice(t * P, (t + 1) * P)

            def u_item(slot, b, r, q=None, part=None, sums=None):
                if part != 1:
                    pe.wait_ge(read[b], r)
                for k in {None: range(KD), 0: range(KD // 2), 1: range(KD // 2, KD)}[part]:
                    if q is not None and b % 2 == 0:
                        pe.wait_ge(u_made, 16 * q + 8 * (b // 2) + k + 1)
                    if sums is not None and k == KD - 2:
                        sum_out(sums, 1)
                    mm = product(b, slot, KD, k, tile_cols(b), u_hi, u_lo, k, k == 0, k == KD - 1)
                if part != 0:
                    mm.then_inc(full[b], 1)

            def sum_h(q, g):
                for t in range(KD):
                    pe.wait_ge(h_sq, 16 * q + 8 * g + t + 1)
                    pe.matmul(sum_pre[g][:, 0:TG], ones, sqh[t % 4], start=t == 0,
                              stop=t == KD - 1).then_inc(h_summed, 1)

            def sum_out(p, g):
                pe.wait_ge(acc_added, out_at(p, DNS - 1, 2 * g + 1) + 1)
                pe.matmul(sum_post[g][:, 0:TG], ones, acc[:, g, :], start=True, stop=True).then_inc(post_summed, 1)

            def keep_clock(n):
                for t in range(n):
                    pe.matmul(sum_post[0][:, 0:TG], ones, h[:, t % KD, tg(0)], start=True, stop=True)

            def first_chunks(q, n, r):
                keep_clock(7)
                pe.wait_ge(lo_made, n + 1)
                u_item(n % 2, 0, r, q, sums=q - 1)
                u_item(n % 2, 1, r, q)
                pe.wait_ge(lo_made, n + 2)
                u_item((n + 1) % 2, 0, r + 1)
                sum_h(q, 1)
                u_item((n + 1) % 2, 1, r + 1)
                for c in range(2):
                    for b in (2, 3):
                        u_item((n + c) % 2, b, r + c, None if c else q)

            def ffn_up(q, n0, r0):
                if q:
                    first_chunks(q, n0, r0)
                else:
                    for c in range(2):
                        pe.wait_ge(lo_made, n0 + c + 1)
                        for b in range(4):
                            u_item(c, b, r0 + c, None if c else q)
                with pe.Fori(1, UPS) as i:
                    for s in range(2):
                        pe.wait_ge(lo_made, n0 + 1 + s + 2 * i)
                        for b in range(4):
                            u_item(s, b, r0 + s + 2 * i)

            def down_item(slot, b, r, kc, sums=None):
                if kc == 0:
                    pe.wait_ge(read[b], r)
                ks = min(KD, KF - KD * kc)
                for k in range(ks):
                    if k == ks // 2 and sums is not None:
                        sum_out(sums, 0)
                    mm = product(b, slot, KD, k, tile_cols(b), hid_hi, hid_lo, KD * kc + k,
                                 kc == 0 and k == 0, kc == KC - 1 and k == ks - 1)
                if kc == KC - 1:
                    mm.then_inc(full[b], 1)
                elif b == 3:
                    mm.then_inc(part_used, 1)

            def down_waits(p, n, kc):
                pe.wait_ge(lo_made, n + 1)
                made = 4 * UPS * (0 if p == 0 else 1)
                pe.wait_ge(hid_made, made + min(2 * KD * (kc + 1), 4 * UPS))

            def ffn_down(p, n0, r0):
                def chunk(slot, n, r, kc):
                    down_waits(p, n, kc)
                    for b in range(4):
                        down_item(slot, b, r, kc)

                with pe.Fori(0, DNS // 2 - 1) as i:
                    for j in range(2 * KC):
                        chunk(j % 2, n0 + j + 2 * KC * i, r0 + j // KC + 2 * i, j % KC)
                n1, r1 = n0 + 2 * KC * (DNS // 2 - 1), r0 + DNS - 2
                for j in range(2 * KC - 2):
                    chunk(j % 2, n1 + j, r1 + j // KC, j % KC)
                for j in (2 * KC - 2, 2 * KC - 1):
                    down_waits(p, n1 + j, j % KC)
                    for b in (0, 1):
                        down_item(j % 2, b, r1 + 1, j % KC)
                down_item(0, 2, r1 + 1, KC - 2, sums=p)
                down_item(0, 3, r1 + 1, KC - 2)
                down_item(1, 2, r1 + 1, KC - 1)
                if p < 2:
                    sum_h(p + 1, 0)
                down_item(1, 3, r1 + 1, KC - 1)

            pe.wait_ge(cst_in, 16)
            sum_h(0, 0)
            sum_h(0, 1)
            ffn_up(0, FFN1, R_FFN1)
            ffn_down(0, FFN1 + 2 * UPS, R_FFN1 + 2 * UPS)

            def turn_v(n):
                r = R_QKV + (6 + n if n < 3 else 10 + n)
                pe.wait_ge(read[3], r + 1)
                for t in range(2):
                    if n == 4:
                        pe.wait_ge((a_pt_act, a_lo)[t], 16)
                    elif n == 3:
                        pe.wait_ge((a_pt_act, a_lo)[t], 13 - t)
                    elif n:
                        pe.wait_ge(v_placed, 3 * n)
                    for blk in range(NB):
                        src = vt[:, t, blk:SEQ:4] if n in (1, 2) else vt[:, t, blk * P:(blk + 1) * P]
                        mm = pe.transpose((tb, ob)[t][:, blk * P:(blk + 1) * P], src, ident)
                    mm.then_inc(v_turned, 1)

            def turn_v_samples(n):
                pe.wait_ge(v_placed, 3 * n + 1)
                for t in range(2):
                    mm = pe.transpose(tb[0:DEC, t * P:(t + 1) * P], vt[:, t, SEQ:T], ident)
                mm.then_inc(v_turned, 1)

            first_chunks(1, QKV, R_QKV)
            for c in range(2, 9):
                pe.wait_ge(lo_made, QKV + c + 1)
                for b in range(4):
                    u_item((QKV + c) % 2, b, R_QKV + c)
                    if b == 0 and c > 6:
                        turn_v(c - 7)
                    if b == 1 and c > 6:
                        turn_v_samples(c - 7)

            def a_scores(u):
                r, hd = divmod(u, AH)
                t, po = hd // 2, 64 * (hd % 2)
                rows = slice(po, po + 64)
                if u:
                    pe.wait_ge(a_biased, 3 * u)
                    pe.wait_ge(a_pt_dve, u - 1)
                pe.matmul(s1[:], q_a[rows, t, r:SEQ:4], k_a[rows, t, 0:SEQ], start=True, stop=True)
                pe.matmul(s2[:, 0:P], q_a[rows, 2 + t, r:SEQ:4], k_a[rows, 2 + t, r:SEQ:4], start=True, stop=True)
                pe.matmul(s2[:, P:2 * P], q_a[rows, 4 + t, r:SEQ:4], k_a[rows, 4 + t, r:SEQ:4], start=True,
                          stop=True).then_inc(a_scored, 1)

            def a_turn(u):
                pe.wait_ge(a_prob, u + 1)
                pe.wait_ge(a_pt_act, u)
                pe.wait_ge(v_placed, 9 + 2 * (u >= 13))
                pe.wait_ge(a_biased, 3 * min(u + 2, 16))
                for n in range(6):
                    dst = tb[:, n * P:(n + 1) * P] if n < 4 else s2[:, (n - 2) * P:(n - 1) * P]
                    mm = pe.transpose(dst, sc[:, u % 2, n * P:(n + 1) * P], ident)
                mm.then_inc(a_turned, 1)

            def a_apply(u):
                r, hd = divmod(u, AH)
                po = 64 * (hd % 2)
                pe.wait_ge(a_pt_act, u + 1)
                pe.wait_ge(a_pt_dve, u + 1)
                pe.wait_ge(a_lo, u)
                for n in range(6):
                    g, blk = (0, n) if n < 4 else (n - 3, r)
                    col = g * 256 + hd * DH
                    mm = pe.matmul(ob[po:po + 64, 0:P], v_a[:, blk, col:col + DH], p_t[:, u % 2, n * P:(n + 1) * P],
                                   start=n == 0, stop=n == 5)
                mm.then_inc(a_out, 1)

            pe.wait_ge(read[3], R_QKV + 6)
            a_scores(0)
            for u in range(16):
                if u + 1 < 16:
                    a_scores(u + 1)
                for j, part in (divmod(x, 2) for x in range(3 * u, 3 * u + 3)):
                    if j % 4 == 0 and part == 0:
                        pe.wait_ge(lo_made, QKV + 9 + j // 4 + 1)
                    u_item((QKV + 9 + j // 4) % 2, j % 4, R_QKV + 9 + j // 4, part=part)
                    if part == 1 and j in (0, 20):
                        turn_v(2 if j == 0 else 3)
                if u == 0:
                    turn_v_samples(2)
                a_turn(u)
                if u:
                    a_apply(u - 1)
            def gate_item(j, part=None):
                if j % 4 == 0 and part != 1:
                    pe.wait_ge(lo_made, GA + j // 4 + 1)
                u_item((GA + j // 4) % 2, j % 4, R_GA + j // 4, part=part)

            gate_item(0)
            a_apply(15)

            def b_scores(w):
                hd, i = divmod(w, NB)
                t, po = hd // 2, 64 * (hd % 2)
                n = (i + 1) * P
                if w < 2:
                    pe.wait_ge((a_biased, a_pt_dve)[w], (48, 16)[w])
                else:
                    pe.wait_ge(b_beta, w - 1)
                pe.matmul((s1, s2)[w % 2][:, 0:n], q_b[po:po + 64, t, i * P:n], k_b[po:po + 64, t, 0:n],
                          start=True, stop=True).then_inc(b_scored, 1)

            def b_turn(w):
                pe.wait_ge(b_weight, w + 1)
                pe.wait_ge(b_wt, w)
                for n in range(w % NB + 1):
                    mm = pe.transpose(tb[:, n * P:(n + 1) * P], beta[:, w % 2, n * P:(n + 1) * P], ident)
                mm.then_inc(b_turned, 1)

            def b_apply(w):
                hd, i = divmod(w, NB)
                po = 64 * (hd % 2)
                pe.wait_ge(b_wt, w + 1)
                pe.wait_ge(b_lo, w)
                for n in range(i + 1):
                    mm = pe.matmul(ob[po:po + 64, 0:P], v_b[:, n, hd * DH:(hd + 1) * DH],
                                   w_t[:, w % 2, n * P:(n + 1) * P], start=n == 0, stop=n == i)
                mm.then_inc(b_out, 1)

            b_scores(0)
            gate_item(1)
            for w in range(32):
                if w + 1 < 32:
                    b_scores(w + 1)
                gate_item(2 + w // 2, w % 2)
                if w == 0:
                    turn_v(4)
                    pe.wait_ge(v_placed, 13)
                b_turn(w)
                if w:
                    b_apply(w - 1)
            b_apply(31)

            def sample_keys_a(x):
                pe.wait_ge(ring_in[x % 4], 16 * (x // 4 + 1))
                pe.wait_ge(self_in, 3 * (x + 1))
                slot, row, rnd = ring[x % 4], 32 * (x % 4), x // 4
                for g, (k0, k1) in enumerate(((0, 129), (129, 194), (194, 211))):
                    for t in range(2):
                        mm = pe.matmul(s1[row:row + AH, rnd * 211 + k0:rnd * 211 + k1], qz_a[:, 2 * g + t, x, :],
                                       slot[:, t * 211 + k0:t * 211 + k1], start=t == 0, stop=t == 1)
                mm.then_inc(ring_used, 1)

            def sample_keys_b(y):
                pe.wait_ge(ring_in[y % 4] if y >= 8 else page_in[y], 16 * (y // 4 + 1) if y >= 8 else 16)
                slot = ring[y % 4] if y >= 8 else blocks[4 + y]
                b, pgi = divmod(y, 2)
                row, col = 32 * (b % 4), (b // 4) * 256 + pgi * P
                for t in range(4):
                    mm = pe.matmul(s2[row:row + BH, col:col + P], qz_b[:, t, b, :], slot[:, t * P:(t + 1) * P],
                                   start=t == 0, stop=t == 3)
                mm.then_inc(ring_used if y >= 8 else page_used, 1)

            def sample_turn_a():
                pe.wait_ge(s_prob, 2)
                pe.wait_ge(b_wt, 32)
                for r in range(2):
                    pe.transpose(tb[:, 2 * r * P:(2 * r + 1) * P], s_a[:, r, 0:P], ident)
                    mm = pe.transpose(tb[0:83, (2 * r + 1) * P:(2 * r + 2) * P], s_a[:, r, P:211], ident)
                mm.then_inc(s_turned, 1)

            def sample_turn_b():
                pe.wait_ge(s_prob, 3)
                pe.wait_ge(b_lo, 32)
                for n in range(4):
                    r, pgi = divmod(n, 2)
                    mm = pe.transpose(ob[:, n * P:(n + 1) * P], s_beta[:, r, pgi * P:(pgi + 1) * P], ident)
                mm.then_inc(s_turned, 1)

            def sample_values_a(b):
                row, rnd = 32 * (b % 4), b // 4
                for t in range(2):
                    cols = slice(row + 2 * t, row + 2 * t + 2)
                    out = s1[row:row + 2, (2 * t + rnd) * P:(2 * t + rnd + 1) * P]
                    pe.matmul(out, pt_a[:, 2 * rnd, cols], va_1[:, b, t * P:(t + 1) * P], start=True, stop=False)
                    mm = pe.matmul(out, pt_a[0:83, 2 * rnd + 1, cols], va_23[:, b, t * P:(t + 1) * P],
                                   start=False, stop=True)
                if b == DEC - 1:
                    mm.then_inc(va_used, 1)

            def sample_values_b(b):
                row, rnd = 32 * (b % 4), b // 4
                for n in range(2):
                    x = 2 * b + n
                    if x < 4:
                        pe.wait_ge(ring_in[x], 16 * 5)
                    elif x < 12:
                        pe.wait_ge(page_in[x - 4], 16 * 2)
                    else:
                        pe.wait_ge(ring_in[x - 12], 16 * 6)
                for t in range(4):
                    cols = slice(row + 2 * t, row + 2 * t + 2)
                    for n in range(2):
                        mm = pe.matmul((s2, ob)[rnd][row:row + 2, t * P:(t + 1) * P], pt_b[:, 2 * rnd + n, cols],
                                       blocks[(2 * b + n) % 12][:, t * P:(t + 1) * P], start=n == 0, stop=n == 1)
                        if b < 2 and t == 3:
                            mm.then_inc(ring_used, 1)
                if b % 4 == 3:
                    mm.then_inc(sb_out, 1)

            def fold_turn(x, dst):
                pe.wait_ge(fold_copied, x + 1)
                for n in range(4):
                    mm = pe.transpose(dst[:, n * P:(n + 1) * P], folded[x][:, n * P:(n + 1) * P], ident)
                mm.then_inc(fold_turned, 1)

            pe.wait_ge(s_zero, 2)
            pe.wait_ge(qz_made, 20)
            y = 0
            for j in range(2, 16):
                gate_item(16 + j)
                if j < 4:
                    for x in range(4 * (j - 2), 4 * (j - 2) + 4):
                        sample_keys_a(x)
                elif j < 9:
                    for _ in range(3 if j < 8 else 4):
                        sample_keys_b(y)
                        y += 1
                if j == 6:
                    sample_turn_a()
                if j == 9:
                    pe.wait_ge(s_pt, 2)
                    pe.wait_ge(va_in, 96)
                if j in (9, 10):
                    for b in range(4 * (j - 9), 4 * (j - 9) + 4):
                        sample_values_a(b)
                if j == 11:
                    sample_turn_b()
                if j == 12:
                    fold_turn(0, tb)
                    pe.wait_ge(s_pt, 3)
                if j >= 12:
                    for b in range(2 * (j - 12), 2 * (j - 12) + 2):
                        sample_values_b(b)
            fold_turn(1, s1)

            pe.wait_ge(s_lo, 2)
            pe.wait_ge(lo_made, PA + 1)
            for x in range(16):
                r, b = divmod(x, 4)
                col = (2 * r + b % 2) * P
                if x == 2:
                    fold_turn(2, s2)
                pe.wait_ge(read[b], R_PA + r)
                for k in range(2):
                    mm = product(b, PA % 2, 2, k, slice(col, col + P), oa_hi, oa_lo, k, k == 0, k == 1)
                mm.then_inc(full[b], 1)
            for x in range(16):
                r, b = divmod(x, 4)
                n, col = PB + r // 2, (2 * (r % 2) + b % 2) * P
                if x == 0:
                    pe.wait_ge(s_lo, 6)
                if x % 8 == 0:
                    pe.wait_ge(lo_made, n + 1)
                pe.wait_ge(read[b], R_PB + r)
                for k in range(4):
                    mm = product(b, n % 2, 4, k, slice(col, col + P), ob_hi, ob_lo, k, k == 0, k == 3)
                mm.then_inc(full[b], 1)

            def wo_item(r, b, sums=False):
                pe.wait_ge(read[b], R_WO + r)
                for k in range(KD):
                    if r == 0:
                        pe.wait_ge(m_made, 4 * (k // 2) + 2 * (b // 2) + k % 2 + 1)
                    if k == KD // 2 and sums:
                        sum_out(1, 0)
                    mm = product(b, (WO + r) % 2, KD, k, tile_cols(b), m_hi, m_lo, k, k == 0, k == KD - 1)
                mm.then_inc(full[b], 1)

            for r in range(DNS):
                pe.wait_ge(lo_made, WO + r + 1)
                for b in range(4 if r < DNS - 2 else 2):
                    wo_item(r, b)
            wo_item(DNS - 2, 2, sums=True)
            wo_item(DNS - 2, 3)
            wo_item(DNS - 1, 2)
            sum_h(2, 0)
            wo_item(DNS - 1, 3)
            ffn_up(2, FFN2, R_FFN2)
            ffn_down(2, FFN2 + 2 * UPS, R_FFN2 + 2 * UPS)
            sum_out(2, 1)


def _chunk(w, rows, cols):
    import numpy as np
    k = (rows.stop - rows.start) // P
    c = w[rows, cols].reshape(k, P, cols.stop - cols.start).transpose(1, 0, 2).reshape(P, -1)
    if c.shape[1] < CH:
        c = np.concatenate([c, np.zeros((P, CH - c.shape[1]), c.dtype)], axis=1)
    return c


def _stream(gate, up, down, w_in, p_a, p_b, w_o, gate2, up2, down2):
    import numpy as np
    every = slice(0, D)

    def ffn(wg, wu, wd):
        for j in range(UPS):
            for w in (wg, wu):
                yield _chunk(w, every, slice(j * CW, (j + 1) * CW))
        for j in range(DNS):
            for kc in range(KC):
                yield _chunk(wd, slice(kc * D, min((kc + 1) * D, FF)), slice(j * CW, (j + 1) * CW))

    chunks = list(ffn(gate, up, down))
    chunks += [_chunk(w_in, every, slice(j * CW, (j + 1) * CW)) for j in range(w_in.shape[1] // CW)]
    chunks.append(_chunk(p_a, slice(0, 256), every))
    chunks += [_chunk(p_b, slice(0, WB), slice(j * 512, (j + 1) * 512)) for j in range(2)]
    chunks += [_chunk(w_o, every, slice(j * CW, (j + 1) * CW)) for j in range(DNS)]
    chunks += list(ffn(gate2, up2, down2))
    return np.stack(chunks)


def _tables():
    import numpy as np
    a = np.arange(P)[:, None]
    d1 = 4 * a - (np.arange(515)[None, :] - 3)
    d1 = np.where((d1 >= 0) & (d1 <= P), d1, FAR)
    d = 4 * (a - np.arange(P)[None, :])
    d2 = np.where(d >= 0, d, FAR)
    d3 = np.where((d >= 0) & (d % 16 == 0), d, FAR)
    tri = (np.arange(P)[None, :] < a).astype(np.float64)
    consts = np.concatenate([np.eye(P), np.ones((P, P)), d1, d2, d3, tri], axis=1).astype(np.float32)
    dist = [128.0 - np.arange(128), [0.0], 256.0 - 4.0 * np.arange(64), [0.0], 256.0 - 16.0 * np.arange(16), [0.0]]
    group = np.repeat([0, 0, 1, 1, 2, 2], [len(x) for x in dist])
    dist = np.concatenate(dist)
    bias = np.zeros((P, 2, 211), np.float32)
    for j in range(4):
        for hd in range(AH):
            bias[32 * j + hd] = [-slope(g, hd) * x for g, x in zip(group, dist)]
    return consts, bias.reshape(P, 422)


def kernel(x_prompt, x_sample, cache_a1_kv, cache_a2_kv, cache_a3_kv, cache_b_kv, page_table,
           g_ffn1_pre, g_ffn1_post, w1_gate, w1_up, w1_down, g_mix_pre, g_mix_post, w_in, b_sb,
           p_a, p_b, w_o, g_ffn2_pre, g_ffn2_post, w2_gate, w2_up, w2_down):
    import numpy as np
    import concourse.bacc as bacc
    from concourse.bass_utils import run_bass_kernel_spmd

    n = {k: np.asarray(v) for k, v in locals().items() if k not in ("np", "bacc", "run_bass_kernel_spmd")}
    x = np.concatenate([n["x_prompt"][0], n["x_sample"][:, 0]], axis=0)
    gains = np.stack([n[k][0] for k in ("g_ffn1_pre", "g_ffn1_post", "g_mix_pre", "g_mix_post", "g_ffn2_pre",
                                        "g_ffn2_post")])
    b_rows = n["b_sb"][0]
    consts, sample_bias = _tables()
    gap = np.zeros((DEC, 1, AH * DH), np.float32)
    rows = [c[0][:, ::s] for c, s in ((n["cache_a1_kv"], 1), (n["cache_a2_kv"], 4), (n["cache_a3_kv"], 16))]
    keys = [r[:, :, 0].reshape(DEC, -1, AH * DH) for r in rows]
    vals = [r[:, :, 1].reshape(DEC, -1, AH * DH) for r in rows]
    ka = np.concatenate([keys[0], gap, keys[1], gap, keys[2], gap], axis=1)
    ka = ka.reshape(DEC, 211, 2, P).transpose(0, 3, 2, 1).reshape(DEC, P, 422)
    pool = n["cache_b_kv"][0]
    n_phys = pool.shape[0]
    kb = pool[:, :, 0].reshape(n_phys, P, 4, P).transpose(0, 3, 2, 1).reshape(n_phys, P, 512)
    arrays = {
        "w_stream": _stream(*(n[k][0] for k in ("w1_gate", "w1_up", "w1_down", "w_in", "p_a", "p_b", "w_o",
                                                "w2_gate", "w2_up", "w2_down"))),
        "x_t": x.reshape(T, KD, P).transpose(2, 1, 0),
        "gains_in": gains.reshape(6, KD, P).transpose(2, 0, 1),
        "b_rows": np.concatenate([np.tile(b_rows, (P, 1)), np.tile(b_rows, P // BH)[:, None]], axis=1),
        "consts": consts,
        "sample_bias": sample_bias,
        "ka_cache": ka,
        "va_cache1": vals[0].transpose(1, 0, 2),
        "va_cache2": np.concatenate([vals[1], vals[2]], axis=1).transpose(1, 0, 2),
        "kb_pool": kb,
        "vb_pool": pool[:, :, 1].reshape(n_phys, P, 512),
        "pages": n["page_table"].reshape(1, -1),
    }
    outs = {
        "y_t": (P, KD, T), "ka1_t": (P, 2, P + DEC), "ka2_t": (P, 2, T), "ka3_t": (P, 2, T), "kb_t": (P, 4, T),
        "va1_o": (P, 256), "va2_o": (P, NB, 256), "va3_o": (P, NB, 256), "vb_o": (P, NB, 512), "vs_t": (P, 10, DEC),
    }
    nc = bacc.Bacc("TRN2", target_bir_lowering=False, num_devices=1)
    arrays = {k: np.ascontiguousarray(v) for k, v in arrays.items()}
    args = [nc.dram_tensor(k, a.shape, mybir.dt.from_np(a.dtype), kind="ExternalInput").ap() for k, a in arrays.items()]
    args += [nc.dram_tensor(k, s, F32, kind="ExternalOutput").ap() for k, s in outs.items()]
    step_program(nc, *args)
    o = run_bass_kernel_spmd(nc, [arrays], core_ids=[0]).results[0]
    o = {k: np.asarray(o[k]) for k in outs}

    def rows_of(t):
        return t.transpose(2, 1, 0).reshape(t.shape[2], -1)

    y = rows_of(o["y_t"])
    result = [y[None, :SEQ], y[SEQ:, None]]
    vs = rows_of(o["vs_t"])
    values = [o["va1_o"], o["va2_o"].reshape(SEQ, 256), o["va3_o"].reshape(SEQ, 256)]
    for g in range(AG):
        k = rows_of(o[f"ka{g + 1}_t"])
        past = k.shape[0] - DEC
        both = np.stack([k[:past], values[g]], axis=1).reshape(1, 1, past, 2, AH, DH)
        new = np.stack([k[past:], vs[:, g * 256:(g + 1) * 256]], axis=1).reshape(1, DEC, 1, 2, AH, DH)
        result += [both, new]
    k = rows_of(o["kb_t"])
    v = o["vb_o"].transpose(1, 0, 2).reshape(SEQ, 512)
    result.append(np.stack([k[:SEQ], v], axis=1).reshape(1, 1, NB, P, 2, BH, DH))
    result.append(np.stack([k[SEQ:], vs[:, 768:]], axis=1).reshape(1, DEC, 1, 2, BH, DH))
    return tuple(result)
```
